# Optimizing a Trainium2 kernel written in Bass

```python
import jax, jax.numpy as jnp
from jax import lax
import numpy as np

D_MODEL = 1024
BATCH = 1
SEQ = 1024
DEPTH = 1

GRID_W = 64
HEAD_DIM = 64
NA_HEADS = 4
NA_ROWS_MAX = 8
NA_COLS = 16
SWA_Q_HEADS = 8
SWA_KV_HEADS = 2
SWA_WINDOW = 128
SWA_BLOCK = 128
POOL_WINDOWS = (2, 4, 8, 16)
POOL_GROUP_DIM = 64
D_A = NA_HEADS * HEAD_DIM
D_B = SWA_Q_HEADS * HEAD_DIM
D_BKV = SWA_KV_HEADS * HEAD_DIM
D_C = len(POOL_WINDOWS) * POOL_GROUP_DIM
D_MIX = D_A + D_B + D_C
D_IN = 3 * D_A + D_B + 2 * D_BKV + D_C
N_GROUPS = 4
EXPERTS_PER_GROUP = 8
N_EXPERTS = N_GROUPS * EXPERTS_PER_GROUP
TOP_K_INNER = 2
D_EXPERT = 256
RMS_EPS = 1e-6

kernel_name = 'hybrid_natten_swa_pool_hmoe_encoder'

def rmsnorm(x, g):
    xf = x.astype(jnp.float32)
    y = xf * lax.rsqrt(jnp.mean(xf * xf, axis=-1, keepdims=True) + RMS_EPS)
    return (y * g.astype(jnp.float32)).astype(x.dtype)

def alibi_slopes(n):
    return (2.0 ** (-8.0 * np.arange(1, n + 1) / n)).astype(np.float32)

def neighbourhood_attention(q, k, v, rel_bias):
    B, S, H, Dh = q.shape
    rows = S // GRID_W
    kr = min(NA_ROWS_MAX, rows)

    def to_grid(a):
        return a.reshape(B, rows, GRID_W, H, Dh).transpose(0, 3, 1, 2, 4)

    qg, kg, vg = to_grid(q * (Dh ** -0.5)), to_grid(k), to_grid(v)
    cols = np.arange(GRID_W)
    col_start = np.clip(cols - NA_COLS // 2, 0, GRID_W - NA_COLS)
    col_idx = col_start[:, None] + np.arange(NA_COLS)[None, :]
    dc_idx = col_idx - cols[:, None] + (NA_COLS - 1)
    bias_c = rel_bias.astype(jnp.float32)[:, :, dc_idx]

    def row_step(r):
        rs = jnp.clip(r - kr // 2, 0, rows - kr)
        q_r = lax.dynamic_index_in_dim(qg, r, axis=2, keepdims=False)
        k_r = lax.dynamic_slice_in_dim(kg, rs, kr, axis=2)[:, :, :, col_idx]
        v_r = lax.dynamic_slice_in_dim(vg, rs, kr, axis=2)[:, :, :, col_idx]
        dr_idx = rs + jnp.arange(kr) - r + (NA_ROWS_MAX - 1)
        bias = jnp.take(bias_c, dr_idx, axis=1).transpose(0, 2, 1, 3)
        s = jnp.einsum('bhcd,bhrcjd->bhcrj', q_r, k_r).astype(jnp.float32) + bias
        p = jax.nn.softmax(s.reshape(B, H, GRID_W, kr * NA_COLS), axis=-1)
        p = p.reshape(s.shape).astype(v.dtype)
        return jnp.einsum('bhcrj,bhrcjd->bhcd', p, v_r)

    o = lax.map(row_step, jnp.arange(rows))
    return o.transpose(1, 0, 3, 2, 4).reshape(B, S, H * Dh)

def sliding_window_gqa(q, k, v, sink):
    B, S, Hq, Dh = q.shape
    Hkv = k.shape[2]
    rep = Hq // Hkv
    nb = S // SWA_BLOCK
    qb = (q * (Dh ** -0.5)).reshape(B, nb, SWA_BLOCK, Hkv, rep, Dh)
    pad = ((0, 0), (SWA_BLOCK, SWA_BLOCK), (0, 0), (0, 0))
    kp, vp = jnp.pad(k, pad), jnp.pad(v, pad)

    def band(a):
        return jnp.concatenate(
            [a[:, i * SWA_BLOCK: i * SWA_BLOCK + S].reshape(B, nb, SWA_BLOCK, Hkv, Dh) for i in range(3)],
            axis=2)

    kb, vb = band(kp), band(vp)
    qi = np.arange(SWA_BLOCK)
    ki = np.arange(3 * SWA_BLOCK)
    diff = ki[None, :] - qi[:, None] - SWA_BLOCK
    kpos = (np.arange(nb)[:, None] - 1) * SWA_BLOCK + ki[None, :]
    valid = (np.abs(diff) <= SWA_WINDOW)[None] & ((kpos >= 0) & (kpos < S))[:, None, :]
    slopes = jnp.asarray(alibi_slopes(Hq)).reshape(Hkv, rep)
    alibi = -slopes[:, :, None, None] * jnp.asarray(np.abs(diff).astype(np.float32))
    s = jnp.einsum('bnqgrd,bnkgd->bngrqk', qb, kb).astype(jnp.float32)
    s = jnp.where(jnp.asarray(valid)[None, :, None, None], s + alibi, -jnp.inf)
    sink_logit = jnp.broadcast_to(sink.astype(jnp.float32).reshape(Hkv, rep, 1, 1),
                                  (B, nb, Hkv, rep, SWA_BLOCK, 1))
    p = jax.nn.softmax(jnp.concatenate([s, sink_logit], axis=-1), axis=-1)[..., :-1].astype(v.dtype)
    o = jnp.einsum('bngrqk,bnkgd->bnqgrd', p, vb)
    return o.reshape(B, S, Hq * Dh)

def multiscale_pool(u, pool_w, pool_scale):
    B, S, C = u.shape
    uf = u.astype(jnp.float32)
    csum = jnp.concatenate([jnp.zeros((B, 1, C), jnp.float32), jnp.cumsum(uf, axis=1)], axis=1)
    t = np.arange(S)
    outs = []
    for gi, w in enumerate(POOL_WINDOWS):
        sl = slice(gi * POOL_GROUP_DIM, (gi + 1) * POOL_GROUP_DIM)
        lo = np.clip(t - w // 2, 0, S)
        hi = np.clip(t + w // 2, 0, S)
        c = csum[:, :, sl]
        cnt = jnp.asarray((hi - lo).astype(np.float32))[None, :, None]
        d = ((c[:, hi] - c[:, lo]) / cnt - uf[:, :, sl]).astype(u.dtype)
        outs.append(d @ pool_w[gi])
    return jnp.concatenate(outs, axis=-1) * pool_scale

def hierarchical_moe(h, rg_w, rg_b, re_w, re_b, e_gate, e_up, e_down):
    B, S, D = h.shape
    t = h.reshape(-1, D)
    g_prob = jax.nn.softmax((t @ rg_w).astype(jnp.float32) + rg_b.astype(jnp.float32), axis=-1)
    g_top_p, g_top = lax.top_k(g_prob, 1)
    e_logits = ((t @ re_w).astype(jnp.float32) + re_b.astype(jnp.float32)).reshape(-1, N_GROUPS, EXPERTS_PER_GROUP)
    e_sel = jnp.take_along_axis(e_logits, g_top[:, :, None], axis=1)[:, 0]
    e_top_p, e_top = lax.top_k(jax.nn.softmax(e_sel, axis=-1), TOP_K_INNER)
    gates = g_top_p * e_top_p / jnp.sum(e_top_p, axis=-1, keepdims=True)
    expert_id = g_top * EXPERTS_PER_GROUP + e_top
    combine = jnp.sum(jax.nn.one_hot(expert_id, N_EXPERTS, dtype=jnp.float32) * gates[..., None], axis=1)
    combine = combine.astype(t.dtype)
    out = jnp.zeros_like(t)
    for e in range(N_EXPERTS):
        y = (jax.nn.silu(t @ e_gate[e]) * (t @ e_up[e])) @ e_down[e]
        out = out + combine[:, e:e + 1] * y
    return out.reshape(B, S, D)

def hybrid_layer(x, norm1_g, w_in, nat_bias, swa_sink, pool_w, pool_scale, w_out,
                 norm2_g, rg_w, rg_b, re_w, re_b, e_gate, e_up, e_down):
    B, S, _ = x.shape
    h = rmsnorm(x, norm1_g)
    proj = h @ w_in
    splits = [int(v) for v in np.cumsum([D_A, D_A, D_A, D_B, D_BKV, D_BKV])]
    aq, ak, av, bq, bk, bv, cu = jnp.split(proj, splits, axis=-1)
    na = lambda a: a.reshape(B, S, NA_HEADS, HEAD_DIM)
    o_a = neighbourhood_attention(na(aq), na(ak), na(av), nat_bias)
    o_b = sliding_window_gqa(bq.reshape(B, S, SWA_Q_HEADS, HEAD_DIM),
                             bk.reshape(B, S, SWA_KV_HEADS, HEAD_DIM),
                             bv.reshape(B, S, SWA_KV_HEADS, HEAD_DIM), swa_sink)
    o_c = multiscale_pool(cu, pool_w, pool_scale)
    x = x + jnp.concatenate([o_a, o_b, o_c], axis=-1) @ w_out
    x = x + hierarchical_moe(rmsnorm(x, norm2_g), rg_w, rg_b, re_w, re_b, e_gate, e_up, e_down)
    return x

def setup_inputs(seed: int = 0) -> dict:
    key = jax.random.key(seed)
    ks = jax.random.split(key, 17)
    n = jax.random.normal
    f32 = jnp.float32
    return {
        'x': n(ks[0], (BATCH, SEQ, D_MODEL), f32),
        'norm1_g': 1.0 + 0.05 * n(ks[1], (DEPTH, D_MODEL), f32),
        'w_in': n(ks[2], (DEPTH, D_MODEL, D_IN), f32) * D_MODEL ** -0.5,
        'nat_bias': 0.2 * n(ks[3], (DEPTH, NA_HEADS, 2 * NA_ROWS_MAX - 1, 2 * NA_COLS - 1), f32),
        'swa_sink': n(ks[4], (DEPTH, SWA_Q_HEADS), f32),
        'pool_w': n(ks[5], (DEPTH, len(POOL_WINDOWS), POOL_GROUP_DIM, POOL_GROUP_DIM), f32) * POOL_GROUP_DIM ** -0.5,
        'pool_scale': 1.0 + 0.1 * n(ks[6], (DEPTH, D_C), f32),
        'w_out': n(ks[7], (DEPTH, D_MIX, D_MODEL), f32) * D_MIX ** -0.5,
        'norm2_g': 1.0 + 0.05 * n(ks[8], (DEPTH, D_MODEL), f32),
        'router_g_w': n(ks[9], (DEPTH, D_MODEL, N_GROUPS), f32) * D_MODEL ** -0.5,
        'router_g_b': 0.01 * n(ks[10], (DEPTH, N_GROUPS), f32),
        'router_e_w': n(ks[11], (DEPTH, D_MODEL, N_EXPERTS), f32) * D_MODEL ** -0.5,
        'router_e_b': 0.01 * n(ks[12], (DEPTH, N_EXPERTS), f32),
        'expert_w_gate': n(ks[13], (DEPTH, N_EXPERTS, D_MODEL, D_EXPERT), f32) * D_MODEL ** -0.5,
        'expert_w_up': n(ks[14], (DEPTH, N_EXPERTS, D_MODEL, D_EXPERT), f32) * D_MODEL ** -0.5,
        'expert_w_down': n(ks[15], (DEPTH, N_EXPERTS, D_EXPERT, D_MODEL), f32) * D_EXPERT ** -0.5,
        'final_g': 1.0 + 0.05 * n(ks[16], (D_MODEL,), f32),
    }

def reference(x, norm1_g, w_in, nat_bias, swa_sink, pool_w, pool_scale, w_out, norm2_g,
              router_g_w, router_g_b, router_e_w, router_e_b, expert_w_gate, expert_w_up,
              expert_w_down, final_g):
    for l in range(DEPTH):
        x = hybrid_layer(x, norm1_g[l], w_in[l], nat_bias[l], swa_sink[l], pool_w[l], pool_scale[l],
                         w_out[l], norm2_g[l], router_g_w[l], router_g_b[l], router_e_w[l],
                         router_e_b[l], expert_w_gate[l], expert_w_up[l], expert_w_down[l])
    return rmsnorm(x, final_g)


_drawn_inputs = setup_inputs


def setup_inputs(seed=0):
    import zlib

    import numpy as np

    out = dict(_drawn_inputs(seed))
    spreads = {}
    factors = {'swa_sink': 2.83, 'router_g_b': 3.567, 'router_e_b': 5.039}
    for name, (base, spread) in spreads.items():
        noise = np.random.default_rng([zlib.crc32(name.encode()), seed]).standard_normal(out[name].shape)
        drawn = base * np.exp(spread * noise) if base else spread * noise
        out[name] = __import__('jax').numpy.asarray(drawn.astype(out[name].dtype))
    for name, factor in factors.items():
        out[name] = (out[name] * factor).astype(out[name].dtype)
    return out
```

```python
from contextlib import ExitStack

import numpy as np

import concourse.bass as bass
from concourse import mybir

ALU = mybir.AluOpType
ACT = mybir.ActivationFunctionType
F32 = mybir.dt.float32
F32R = mybir.dt.float32r
I32 = mybir.dt.int32
U32 = mybir.dt.uint32
AX_X = mybir.AxisListType.X

P = 128
D = 1024
S = 1024
TT = S // P
KT = D // P
HD = 64
GRID_W = 64
ROWS = S // GRID_W
NA_HEADS, NA_ROWS, NA_COLS = 4, 8, 16
SWA_HEADS, SWA_KV, WINDOW = 8, 2, 128
POOL_WINDOWS = (2, 4, 8, 16)
PAD = 8
D_IN = 3 * NA_HEADS * HD + SWA_HEADS * HD + 2 * SWA_KV * HD + len(POOL_WINDOWS) * HD
MT = D_IN // P
N_GROUPS, PER_GROUP, N_EXP, DE = 4, 8, 32, 256
NR = N_GROUPS + N_EXP
EPS = 1e-6
BIG = 1e30
CAP = 80
COLS = 96
N_OVF = (2 * S) // (CAP + 1)
PITCH = 64
NI = 96
LT = N_EXP + N_OVF
NOWHERE = 4096
RING = 4
MAGIC = 12582912.0

POOL_OPS = 16
RD_GROUP, RD_PAIR, RD_COUNTED = 2, 16, 32

ORDER = [4, 0, 5, 1, 11, 2, 3, 6, 7, 8, 9, 10, 12, 13]
V_TILES = [4, 5, 11]
PROJ = [(0, 0), (1, 0), (0, 1), (1, 1)] + [(i, n) for i in range(2, 14) for n in range(2)]
NX = 4


def na_rows(i):
    lo = min(max(2 * i - NA_ROWS // 2, 0), ROWS - NA_ROWS)
    hi = min(max(2 * i + 1 - NA_ROWS // 2, 0), ROWS - NA_ROWS) + NA_ROWS
    return lo, hi - lo


def attention_plan():
    steps = []
    for i in range(TT):
        lo, n = na_rows(i)
        steps.append(("na", i, 0, lo * GRID_W, n * GRID_W))
    for b in range(TT):
        lo, hi = max(b - 1, 0), min(b + 2, TT)
        for g in range(SWA_KV):
            steps.append(("swa", b, g, lo * P, (hi - lo) * P))
    lag = 3
    ticks = [[] for _ in range(4 * len(steps) + lag + 4)]
    for s, (kind, i, g, k0, nk) in enumerate(steps):
        nc_ = -(-nk // P)
        items = []
        for c in range(nc_ + 1):
            if c < nc_:
                items.append(("T", s, c))
            if c > 0 and (kind == "na" or g == 1):
                items.append(("V", s, c - 1))
        for j, it in enumerate(items):
            ticks[4 * s + 3 + lag + (4 * j) // len(items)].append(it)
    return steps, ticks


def encoder(nc, x, norm1_g, w_in, nat_win, swa_sink, pool_w, pool_scale, w_out, norm2_g,
            rg_w, rg_b, re_w, re_b, e_gate, e_up, e_down, final_g,
            c_sq, c_colmask, c_rowmask, c_alibi, c_iedge, c_misc, c_dest, out):
    steps, ticks = attention_plan()
    NU = 4 * len(steps)

    h2_d = nc.dram_tensor("h2_rows", [S, D], F32).ap()
    y_d = nc.dram_tensor("expert_rows", [2 * S, D], F32).ap()

    with ExitStack() as ctx:
        KB = 1024
        arena = ctx.enter_context(nc.sbuf_tensor("arena", [P, 203 * 256 + 160], F32))
        base = nc.sbuf_base - (203 * KB + 640)
        del arena

        def at(name, shape, dt, off):
            return nc.alloc_sbuf_tensor_at(name, shape, dt, offset=base + int(off))

        def sem(name):
            return ctx.enter_context(nc.semaphore(name))

        o = 0
        ident = at("ident", [P, P], F32, o); o += 512
        ones = at("ones", [P, P], F32, o); o += 512
        ut = at("ut", [P, P], F32, o); o += 512
        gbc = at("gbc", [P, D], F32, o); o += 4096
        rw = at("rw", [P, KT, NR], F32, o); o += KT * NR * 4
        rb = at("rb", [P, NR], F32, o); o += 160
        misc = at("misc", [P, 12 + NI], F32, o); o += 448
        nsink = at("nsink", [P, SWA_HEADS], F32, o); o += 32
        pscale = at("pscale", [P, 2], F32, o); o += 32
        stat = at("stat", [P, 4, TT], F32, o); o += 128
        mneg = at("mneg", [P, NU], F32, o); o += 4 * NU
        esum = at("esum", [P, NU], F32, o); o += 4 * NU
        logit = at("logit", [P, TT, NR], F32, o); o += TT * NR * 4
        gates = at("gates", [P, 2, TT], F32, o); o += 64
        pwd = at("pwd", [P, 2, P], F32, o); o += 1024
        colmask = at("colmask", [P, GRID_W], F32, o); o += 256
        rowmask = at("rowmask", [P, 9], F32, o); o += 64
        iedge = at("iedge", [P, 2, 2 * PAD + 2], F32, o); o += 160
        dvals = at("dvals", [P, 2 * TT], F32, o); o += 64
        neg_half = at("neg_half", [P, 1], F32, o); o += 32
        PERSIST = 11 * KB + 128
        assert o <= PERSIST, o
        TD, H, W, Q, V, CU, TMP = PERSIST, 47 * KB, 111 * KB, 135 * KB, 175 * KB, 187 * KB, 195 * KB + 256
        xin = [at(f"xin{i}", [P, D], F32, TD + 4096 * i) for i in range(NX)]
        xn = [at(f"xn{i}", [P, D], F32, TD + 4096 * (NX + i)) for i in range(NX)]
        hThi = at("hThi", [P, KT, S], F32R, H)
        hTlo = at("hTlo", [P, KT, S], F32R, H + 32 * KB)
        wraw = [at(f"wraw{i}", [P, KT, P], F32, W + 4096 * i) for i in range(2)]
        whi = [at(f"whi{i}", [P, KT, P], F32R, W + 8192 + 4096 * i) for i in range(2)]
        wlo = [at(f"wlo{i}", [P, KT, P], F32R, W + 16384 + 4096 * i) for i in range(2)]
        qa = at("qa", [P, 2, S], F32, Q)
        ka = at("ka", [P, 2, S], F32, Q + 8 * KB)
        qb = at("qb", [P, 4, S], F32, Q + 16 * KB)
        kb = at("kb", [P, 2, S], F32, Q + 32 * KB)
        vtok = at("vtok", [P, TT, 3 * P], F32, V)
        cu = at("cu", [P, 2, S + 2 * PAD], F32, CU)
        vT = [at(f"vT{i}", [P, S], F32, TMP + 4096 * i) for i in range(2)]
        NEDGE, NINNER = 14, 9
        te = at("te", [P, NA_HEADS, NEDGE, GRID_W], F32, TD)
        ti = at("ti", [P, NA_HEADS, NINNER, GRID_W], F32, TD + NA_HEADS * NEDGE * GRID_W * 4)
        alibi = at("alibi", [P, SWA_HEADS, 3 * P], F32, TD + NA_HEADS * (NEDGE + NINNER) * GRID_W * 4)
        oT = at("oT", [P, KT, S], F32, H)
        pna = [at(f"pna{i}", [P, 4, 9 * GRID_W], F32, H + 32 * KB + i * 9216) for i in range(3)]
        pswa = [at(f"pswa{i}", [P, 4, 3 * P + 1], F32, H + 32 * KB + off) for i, off in enumerate((18432, 24608, 0, 9216))]
        ptna = [at(f"ptna{i}", [P, 5, 512], F32, W + i * 10 * KB) for i in range(2)]
        ptswa = [at(f"ptswa{i}", [P, 3, 2, 512], F32, W + i * 12 * KB) for i in range(2)]
        pa = at("pa", [P, S + 2 * PAD], F32, TMP)
        pb = at("pb", [P, S + 2 * PAD], F32, TMP + 4160)
        oThi = at("oThi", [P, KT, S], F32R, W)
        oTlo = at("oTlo", [P, KT, S], F32R, W + 32 * KB)
        wohi = [at(f"wohi{n}", [P, KT, 512], F32R, H + 32 * KB * (1 - n)) for n in range(2)]
        wolo = [at(f"wolo{n}", [P, KT, 512], F32R, H + 32 * KB * (1 - n) + 16 * KB) for n in range(2)]
        woraw = [at(f"woraw{i}", [P, 512], F32, V + 2048 * i) for i in range(4)]
        xres = [at(f"xres{i}", [P, 512], F32, V + 8192 + 2048 * i) for i in range(2)]
        x1 = at("x1", [P, TT, D], F32, TD)
        h2 = [at(f"h2{i}", [P, D], F32, CU + 4096 * i) for i in range(2)]
        h2T = [at(f"h2T{i}", [P, KT, P], F32, TMP + 4096 * i) for i in range(2)]
        rt = [at(f"rt{i}", [P, TT, N_EXP], F32, V + 1024 * i) for i in range(8)]
        rs = at("rs", [P, 24, 32], F32, V + 8192)
        place = at("place", [P, 3, 2 * TT], F32, V + 8192 + 3072)
        row_hot = at("row_hot", [P, 2 * TT, CAP], F32, TMP)
        tile_hot = at("tile_hot", [P, 2 * TT, LT], F32, H + 24 * KB)
        eoff = [H + 32 * KB, W, W + 24 * KB, H]
        wg = [at(f"wg{i}", [P, KT, DE], F32, eoff[i]) for i in range(RING)]
        wu = [at(f"wu{i}", [P, KT, DE], F32, eoff[i] + 8 * KB) for i in range(RING)]
        wd = [at(f"wd{i}", [P, 2, D], F32, eoff[i] + 16 * KB) for i in range(RING)]
        pad = at("pad", [CAP, LT], F32, V + 8192 + 3072 + 256)
        dest = at("dest", [CAP, LT], I32, W + 48 * KB)
        tok = at("tok", [CAP, LT], I32, W + 48 * KB + 256)
        tokc = [at(f"tokc{i}", [CAP, 1], I32, W + 48 * KB + 704 + 32 * i) for i in range(2)]
        destc = [at(f"destc{i}", [CAP, 1], I32, W + 48 * KB + 768 + 32 * i) for i in range(2)]
        ovf_cmp = at("ovf_cmp", [P, N_OVF, N_EXP], F32, H + 28 * KB)
        eid = at("eid", [P, 32], I32, W + 48 * KB + 576)
        sg = [at(f"sg{i}", [P, 2, COLS], F32, W + 49 * KB + 768 * i) for i in range(2)]
        hT = [at(f"hT{i}", [P, 2, COLS], F32, W + 51 * KB + 768 * i) for i in range(2)]
        ysb = [at(f"ysb{i}", [CAP, D], F32, W + 53 * KB + 4096 * i) for i in range(2)]
        xg = [at(f"xg{i}", [COLS, D], F32, CU + 4096 * i) for i in range(2)]
        xT = [at(f"xT{i}", [P, KT, COLS], F32, TMP + 3072 * i) for i in range(2)]
        y0 = [at(f"y0{i}", [P, D], F32, H + 8192 * i) for i in range(TT)]
        y1 = [at(f"y1{i}", [P, D], F32, H + 8192 * i + 4096) for i in range(TT)]
        fo = [at(f"fo{i}", [P, D], F32, W + 4096 * i) for i in range(TT)]

        ps = ctx.enter_context(nc.psum_tensor("ps", [P, 8, 512], F32))

        const_in = sem("const_in")
        mats_in = sem("mats_in")
        g_in = sem("g_in")
        x_in = [sem(f"x_in{i}") for i in range(NX)]
        sq_done = sem("sq_done")
        eps_added = sem("eps_added")
        rstd_a = sem("rstd_a")
        xn_done = sem("xn_done")
        xtr_done = sem("xtr_done")
        hi_done = sem("hi_done")
        lo_done = sem("lo_done")
        w_in_s = [sem(f"w_in{i}") for i in range(2)]
        w_split = sem("w_split")
        proj_done = sem("proj_done")
        proj_out = sem("proj_out")
        vtr_done = sem("vtr_done")
        v_ready = sem("v_ready")
        cu_zero = sem("cu_zero")
        tab_in = sem("tab_in")
        cmask_in = sem("cmask_in")
        pc_in = sem("pc_in")
        idx_t = sem("idx_t")
        idx_d = sem("idx_d")
        ti_copied = sem("ti_copied")
        te_ready = sem("te_ready")
        ti_ready = sem("ti_ready")
        sink_set = sem("sink_set")
        score_done = sem("score_done")
        bias_done = sem("bias_done")
        exp_done = sem("exp_done")
        recip_done = sem("recip_done")
        norm_p = sem("norm_p")
        norm_v = sem("norm_v")
        tr_done = sem("tr_done")
        pt_v = sem("pt_v")
        pt_a = sem("pt_a")
        pv_done = sem("pv_done")
        o_out = sem("o_out")
        pool_step = sem("pool_step")
        pool_mm = sem("pool_mm")
        pool_out = sem("pool_out")
        oThi_done = sem("oThi_done")
        oTlo_done = sem("oTlo_done")
        wo_in = [sem(f"wo_in{i}") for i in range(4)]
        wohi_done = [sem(f"wohi_done{n}") for n in range(2)]
        wolo_done = [sem(f"wolo_done{n}") for n in range(2)]
        xr_in = [sem(f"xr_in{i}") for i in range(2)]
        out_mm = sem("out_mm")
        x1_done = sem("x1_done")
        sq2_done = sem("sq2_done")
        rstd_b = sem("rstd_b")
        h2_done = sem("h2_done")
        h2_stored = [sem(f"h2_stored{i}") for i in range(2)]
        h2tr_done = sem("h2tr_done")
        h2T_done = sem("h2T_done")
        logit_mm = sem("logit_mm")
        logit_done = sem("logit_done")
        rd = sem("rd")
        r_exp = sem("r_exp")
        rank_mm = sem("rank_mm")
        pad_set = sem("pad_set")
        one_hots = sem("one_hots")
        list_mm = sem("list_mm")
        tok_done = sem("tok_done")
        wgu_in = [sem(f"wgu_in{i}") for i in range(RING)]
        wd_in = [sem(f"wd_in{i}") for i in range(RING)]
        xg_zero = sem("xg_zero")
        xg_in = [sem(f"xg_in{i}") for i in range(2)]
        etr_done = sem("etr_done")
        xT_done = sem("xT_done")
        gu_done = sem("gu_done")
        silu_done = sem("silu_done")
        hT_done = sem("hT_done")
        down_done = sem("down_done")
        y_a = sem("y_a")
        y_v = sem("y_v")
        y_put = [sem(f"y_put{i}") for i in range(2)]
        v_w = sem("v_w")
        v_idx = sem("v_idx")
        v_x = sem("v_x")
        v_tr = sem("v_tr")
        v_xT = sem("v_xT")
        v_gu = sem("v_gu")
        v_silu = sem("v_silu")
        v_hT = sem("v_hT")
        v_ya = sem("v_ya")
        v_yv = sem("v_yv")
        yc_in = [sem(f"yc_in{i}") for i in range(TT)]
        c_sum = sem("c_sum")
        c_sq_done = sem("c_sq_done")
        c_out = sem("c_out")
        out_put = sem("out_put")

        block = ctx.enter_context(nc.Block())

        chunk_no = {}
        vnum = {}
        for tick in ticks:
            for kind, s, c in tick:
                if kind == "T":
                    chunk_no[(s, c)] = len(chunk_no)
                else:
                    vnum[(s, c)] = len(vnum)
        last_chunk = {s: max(c for (s_, c) in chunk_no if s_ == s) for s in range(len(steps))}
        NA_STEPS = TT
        o_steps = [s for s in range(len(steps)) if steps[s][0] == "na" or steps[s][2] == 1]

        def chunk_ready(eng, n):
            if n >= 0:
                eng.wait_ge(pt_v if n % 2 == 0 else pt_a, n // 2 + 1)

        def norm_by_vector(u):
            return u % 2 == 1

        def all_chunks_before(eng, n):
            for m in (n - 1, n - 2):
                chunk_ready(eng, m)

        def pbuf(u):
            s = u // 4
            if s < NA_STEPS:
                return pna[s % 3][:, u % 4, 0:steps[s][4]]
            return pswa[s % 4][:, u % 4, 1:1 + steps[s][4]]

        def sbank(u):
            return 2 * (u % 2) if u // 4 < NA_STEPS else u % 4

        def put_count(it, v):
            return it * (16 * RING // 2) + 16 * ((v - 2) // 2 + 1)

        def evacuate_chunk(eng, copy, done, s, c):
            n = chunk_no[(s, c)]
            kind, i, g, k0, nk = steps[s]
            w = min(P, nk - c * P)
            eng.wait_ge(tr_done, n + 1)
            if kind == "na":
                if s >= 2:
                    eng.wait_ge(pv_done, vnum[(s - 2, last_chunk[s - 2])] + 1)
                copy(ptna[s % 2][0:w, c, :], ps[0:w, 4 + n % 2, :]).then_inc(done, 1)
            else:
                before = NA_STEPS - 1 if i < 2 else NA_STEPS + 2 * (i - 2) + 1
                eng.wait_ge(pv_done, vnum[(before, last_chunk[before])] + 1)
                copy(ptswa[i % 2][:, c, g, :], ps[:, 4 + n % 2, :]).then_inc(done, 1)

        @block.sync
        def _(sp):
            def load_x(t):
                if t >= NX:
                    sp.wait_ge(xn_done, t - NX + 1)
                sp.dma_start(xin[t % NX][:], x[0, t * P:(t + 1) * P, :]).then_inc(x_in[t % NX], 16)

            def load_w(i):
                m = ORDER[i]
                if i >= 2:
                    sp.wait_ge(w_split, 2 * (i - 1))
                sp.dma_start(wraw[i % 2][:], w_in[0, :, m * P:(m + 1) * P].rearrange("(k p) n -> p k n", p=P)
                             ).then_inc(w_in_s[i % 2], 16)

            load_x(0)
            sp.dma_start(gbc[:], norm1_g.partition_broadcast(P)).then_inc(g_in, 16)
            sp.dma_start(ident[:], c_sq[0]).then_inc(mats_in, 16)
            load_x(1)
            load_w(0)
            for t in range(2, NX):
                load_x(t)
            load_w(1)
            for t in range(NX, TT):
                load_x(t)
            sp.dma_start(ones[:], c_sq[1]).then_inc(const_in, 16)
            sp.dma_start(ut[:], c_sq[2]).then_inc(const_in, 16)
            sp.dma_start(misc[:], c_misc.partition_broadcast(P)).then_inc(const_in, 16)
            sp.dma_start(rb[:, 0:N_GROUPS], rg_b.partition_broadcast(P)).then_inc(const_in, 16)
            sp.dma_start(rb[:, N_GROUPS:NR], re_b.partition_broadcast(P)).then_inc(const_in, 16)
            sp.dma_start(rw[:, :, 0:N_GROUPS], rg_w[0].rearrange("(k p) n -> p k n", p=P)).then_inc(const_in, 16)
            sp.dma_start(rw[:, :, N_GROUPS:NR], re_w[0].rearrange("(k p) n -> p k n", p=P)).then_inc(const_in, 16)
            sp.dma_start(nsink[:], swa_sink.partition_broadcast(P)).then_inc(const_in, 16)
            with nc.allow_non_contiguous_dma(reason="256 scales"):
                sp.dma_start(pscale[:], pool_scale[0].rearrange("(i p) -> p i", p=P)).then_inc(const_in, 16)
            sp.wait_ge(xtr_done, 2 * TT)
            for a in range(2):
                sp.dma_start(te[a * GRID_W:(a + 1) * GRID_W], nat_win[:, :, 1 - a:1 - a + NEDGE, :]).then_inc(tab_in, 16)
            sp.dma_start(alibi[:], c_alibi).then_inc(tab_in, 16)
            for i in range(2, MT):
                load_w(i)
            sp.dma_start(gbc[:], norm2_g.partition_broadcast(P)).then_inc(g_in, 16)

            def load_wo(n, k):
                c = n * KT + k
                if c >= 4:
                    if (c - 4) < KT:
                        sp.wait_ge(wolo_done[0], c - 3)
                    else:
                        sp.wait_ge(wolo_done[1], c - 4 - KT + 1)
                cols = slice(n * 512, (n + 1) * 512)
                dst = woraw[c % 4]
                if 2 <= k < 6:
                    for g in range(2):
                        r0 = 256 + (4 * g + k - 2) * HD
                        sp.dma_start(dst[g * HD:(g + 1) * HD, :], w_out[0, r0:r0 + HD, cols]).then_inc(wo_in[c % 4], 16)
                else:
                    sp.dma_start(dst[:], w_out[0, k * P:(k + 1) * P, cols]).then_inc(wo_in[c % 4], 32)

            def load_xres(g):
                n, t = g // TT, g % TT
                if g >= 2:
                    sp.wait_ge(x1_done, g - 1)
                sp.dma_start(xres[g % 2][:], x[0, t * P:(t + 1) * P, n * 512:(n + 1) * 512]).then_inc(xr_in[g % 2], 16)

            sp.wait_ge(o_out, len(o_steps))
            for k in range(KT):
                load_wo(0, k)
                if k < 2:
                    load_xres(k)
            for k in range(4):
                load_wo(1, k)
            for g in range(2, 8):
                load_xres(g)
                if g < 6:
                    load_wo(1, g + 2)

            def load_expert(e, u, dynamic):
                g_src = e_gate[0, e] if not dynamic else e_gate[0, bass.ds(e, 1)].rearrange("a d f -> (a d) f")
                u_src = e_up[0, e] if not dynamic else e_up[0, bass.ds(e, 1)].rearrange("a d f -> (a d) f")
                d_src = e_down[0, e] if not dynamic else e_down[0, bass.ds(e, 1)].rearrange("a d f -> (a d) f")
                return (g_src.rearrange("(k p) f -> p k f", p=P), u_src.rearrange("(k p) f -> p k f", p=P),
                        d_src.rearrange("(k p) f -> p k f", p=P))

            def fetch_expert(e, u, dynamic=False):
                a, b, c = load_expert(e, u, dynamic)
                sp.dma_start(wg[u][:], a).then_inc(wgu_in[u], 16)
                sp.dma_start(wu[u][:], b).then_inc(wgu_in[u], 16)
                sp.dma_start(wd[u][:], c).then_inc(wd_in[u], 16)

            def store_h2(t):
                sp.wait_ge(h2_done, t + 1)
                sp.dma_start(h2_d[t * P:(t + 1) * P, :], h2[t % 2][:]).then_inc(h2_stored[t % 2], 16)

            sp.wait_ge(out_mm, TT)
            fetch_expert(0, 0)
            for g in range(8, 2 * TT):
                load_xres(g)
                if g >= 10:
                    store_h2(g - 10)
            store_h2(TT - 2)
            store_h2(TT - 1)
            sp.wait_ge(out_mm, 2 * TT)
            for u in range(1, RING):
                fetch_expert(u, u)
            with sp.Fori(1, N_EXP // RING) as it:
                for u in range(RING):
                    sp.wait_ge(down_done, it * RING + (u - RING + 1))
                    fetch_expert(it * RING + u, u, True)
            sp.dma_start(gbc[:], final_g.rearrange("(a d) -> a d", a=1).partition_broadcast(P)).then_inc(g_in, 16)
            sp.wait_ge(down_done, N_EXP)
            n_ovf = sp.value_load(eid[0:1, N_OVF:N_OVF + 1], min_val=0, max_val=N_OVF)
            with sp.If(n_ovf > 0):
                with sp.Fori(0, N_OVF) as j:
                    with sp.If(j < n_ovf):
                        e = sp.value_load(eid[0:1, bass.ds(j, 1)], min_val=0, max_val=N_EXP - 1)
                        a, b, c = load_expert(e, 0, True)
                        sp.wait_ge(down_done, j + N_EXP)
                        sp.dma_start(wg[0][:], a).then_inc(v_w, 16)
                        sp.dma_start(wu[0][:], b).then_inc(v_w, 16)
                        sp.dma_start(wd[0][:], c).then_inc(v_w, 16)

            sp.wait_ge(y_put[1], 16 * (N_EXP // 2))
            sp.wait_ge(y_put[0], n_ovf * 16 + 16 * (N_EXP // 2))

            def load_rows(t):
                sp.dma_start(y0[t][:], y_d[t * P:(t + 1) * P, :]).then_inc(yc_in[t], 16)
                sp.dma_start(y1[t][:], y_d[S + t * P:S + (t + 1) * P, :]).then_inc(yc_in[t], 16)

            def store(t):
                sp.wait_ge(c_out, t + 1)
                sp.dma_start(out[0, t * P:(t + 1) * P, :], fo[t][:]).then_inc(out_put, 16)

            for t in range(TT):
                load_rows(t)
            for t in range(TT):
                store(t)
            sp.wait_ge(out_put, 16 * TT)

        @block.tensor
        def _(pe):
            def x_transposes(t):
                pe.wait_ge(xn_done, t + 1)
                for j in range(2):
                    b = 2 * t + j
                    if b >= 4:
                        pe.wait_ge(lo_done, b - 3)
                    for c in range(4):
                        k = 4 * j + c
                        mm = nc.tensor.transpose(ps[:, b % 4, c * P:(c + 1) * P], xn[t % NX][:, k * P:(k + 1) * P], ident[:])
                    mm.then_inc(xtr_done, 1)

            def project(i, n):
                g = PROJ.index((i, n))
                pe.wait_ge(w_split, 2 * (i + 1))
                pe.wait_ge(lo_done, 8 * (n + 1))
                if g >= 4:
                    pe.wait_ge(proj_out, g - 3)
                bank = ps[:, 4 + g % 4, :]
                cols = slice(n * 512, (n + 1) * 512)
                for k in range(KT):
                    nc.tensor.matmul(bank, whi[i % 2][:, k, :], hThi[:, k, cols], start=(k == 0), stop=False)
                    nc.tensor.matmul(bank, whi[i % 2][:, k, :], hTlo[:, k, cols], start=False, stop=False)
                    mm = nc.tensor.matmul(bank, wlo[i % 2][:, k, :], hThi[:, k, cols], start=False, stop=(k == KT - 1))
                mm.then_inc(proj_done, 1)

            def v_transposes(v):
                pe.wait_ge(proj_out, PROJ.index((2 * v, 1)) + 1)
                for n in range(2):
                    b = 2 * v + n
                    if b >= 4:
                        pe.wait_ge(v_ready, b - 3)
                    for c in range(4):
                        mm = nc.tensor.transpose(ps[:, b % 4, c * P:(c + 1) * P],
                                                 vT[v % 2][:, (4 * n + c) * P:(4 * n + c + 1) * P], ident[:])
                    mm.then_inc(vtr_done, 1)

            pe.wait_ge(mats_in, 16)
            for t in range(4):
                x_transposes(t)
            project(0, 0)
            x_transposes(4)
            x_transposes(5)
            project(1, 0)
            x_transposes(6)
            x_transposes(7)
            for i, n in PROJ[2:]:
                project(i, n)
                if n == 1 and i in (1, 3, 5):
                    v_transposes(i // 2)

            def scores(u):
                s, h = u // 4, u % 4
                kind, i, g, k0, nk = steps[s]
                if s < NA_STEPS:
                    if u >= 2:
                        pe.wait_ge(bias_done, u - 1)
                    q = qa[(h % 2) * HD:(h % 2 + 1) * HD, h // 2, i * P:(i + 1) * P]
                    half = nk // 2
                    for r in range(2):
                        k = ka[(h % 2) * HD:(h % 2 + 1) * HD, h // 2, k0 + r * half:k0 + (r + 1) * half]
                        mm = nc.tensor.matmul(ps[:, sbank(u) + r, 0:half], q, k, start=True, stop=True)
                else:
                    pe.wait_ge(bias_done, max(u - 3, 4 * NA_STEPS))
                    hh = 4 * g + h
                    side = slice((hh % 2) * HD, (hh % 2 + 1) * HD)
                    mm = nc.tensor.matmul(ps[:, sbank(u), 0:nk], qb[side, hh // 2, i * P:(i + 1) * P],
                                          kb[side, g, k0:k0 + nk], start=True, stop=True)
                mm.then_inc(score_done, 1)

            def transposes(s, c):
                n = chunk_no[(s, c)]
                w = min(P, steps[s][4] - c * P)
                if c == 0:
                    pe.wait_ge(norm_p, sum(not norm_by_vector(u) for u in range(4 * s + 4)))
                    pe.wait_ge(norm_v, sum(norm_by_vector(u) for u in range(4 * s + 4)))
                chunk_ready(pe, n - 2)
                for h in range(4):
                    mm = nc.tensor.transpose(ps[0:w, 4 + n % 2, h * P:(h + 1) * P],
                                             pbuf(4 * s + h)[:, c * P:c * P + w], ident[:])
                mm.then_inc(tr_done, 1)

            def times_values(s, c):
                kind, i, g, k0, nk = steps[s]
                oi = o_steps.index(s)
                w = min(P, nk - c * P)
                tile = k0 // P + c
                chunk_ready(pe, chunk_no[(s, c)])
                if c == 0 and oi >= 2:
                    pe.wait_ge(o_out, oi - 1)
                bank = ps[:, 6 + oi % 2, :]
                if kind == "na":
                    for h in range(4):
                        half = slice((h % 2) * HD, (h % 2 + 1) * HD)
                        mm = nc.tensor.matmul(bank[half, (h // 2) * P:(h // 2 + 1) * P],
                                              vtok[0:w, tile, h * HD:(h + 1) * HD], ptna[s % 2][0:w, c, h * P:(h + 1) * P],
                                              start=(c == 0 and h < 2), stop=(c == last_chunk[s]), skip_group_check=True)
                else:
                    chunk_ready(pe, chunk_no[(s - 1, c)])
                    for gg in range(2):
                        mm = nc.tensor.matmul(bank[gg * HD:(gg + 1) * HD, :], vtok[:, tile, 256 + gg * HD:256 + (gg + 1) * HD],
                                              ptswa[i % 2][:, c, gg, :], start=(c == 0), stop=(c == last_chunk[s]))
                mm.then_inc(pv_done, 1)

            def pooled(i, n):
                pe.wait_ge(pool_step, POOL_OPS)
                mm = nc.tensor.matmul(ps[:, 2 * i + n, :], pwd[:, i, :], cu[:, i, PAD + n * 512:PAD + (n + 1) * 512],
                                      start=True, stop=True)
                mm.then_inc(pool_mm, 1)

            pe.wait_ge(v_ready, 6)
            pe.wait_ge(proj_out, 2 * MT)
            pe.wait_ge(const_in, 16 * 9)
            for u, tick in enumerate(ticks):
                if u < NU:
                    scores(u)
                for kind, s, c in tick:
                    (transposes if kind == "T" else times_values)(s, c)
            pe.wait_ge(bias_done, NU)
            for i in range(2):
                for n in range(2):
                    pooled(i, n)

            def out_proj(n, t):
                g = n * TT + t
                pe.wait_ge(oTlo_done, t + 1)
                pe.wait_ge(pool_out, 4)
                if g >= 4:
                    pe.wait_ge(x1_done, g - 3)
                rows = slice(t * P, (t + 1) * P)
                for k in range(KT):
                    if t == 0:
                        pe.wait_ge(wolo_done[n], k + 1)
                    nc.tensor.matmul(ps[:, g % 4, :], oThi[:, k, rows], wohi[n][:, k, :], start=(k == 0), stop=False)
                    nc.tensor.matmul(ps[:, g % 4, :], oThi[:, k, rows], wolo[n][:, k, :], start=False, stop=False)
                    mm = nc.tensor.matmul(ps[:, g % 4, :], oTlo[:, k, rows], wohi[n][:, k, :], start=False, stop=(k == KT - 1))
                mm.then_inc(out_mm, 1)

            def h2_transposes(t):
                pe.wait_ge(h2_done, t + 1)
                if t >= 1:
                    pe.wait_ge(h2T_done, 2 * t)
                for j in range(2):
                    for c in range(4):
                        k = 4 * j + c
                        mm = nc.tensor.transpose(ps[:, 4 + j, c * P:(c + 1) * P], h2[t % 2][:, k * P:(k + 1) * P], ident[:])
                    mm.then_inc(h2tr_done, 1)

            def logits(t):
                pe.wait_ge(h2T_done, 2 * t + 2)
                if t >= 2:
                    pe.wait_ge(logit_done, t - 1)
                for k in range(KT):
                    mm = nc.tensor.matmul(ps[:, 6 + t % 2, 0:NR], h2T[t % 2][:, k, :], rw[:, k, :],
                                          start=(k == 0), stop=(k == KT - 1))
                mm.then_inc(logit_mm, 1)

            for t in range(TT):
                out_proj(0, t)
            for t in range(TT):
                out_proj(1, t)
                if t >= 1:
                    h2_transposes(t - 1)
                if t >= 2:
                    logits(t - 2)
            h2_transposes(TT - 1)
            logits(TT - 2)
            logits(TT - 1)
            pe.wait_ge(rd, RD_COUNTED)
            nc.tensor.matmul(ps[:, 0, 0:TT * N_EXP], ut[:], rt[2][:].rearrange("p t e -> p (t e)"), start=True, stop=False)
            nc.tensor.matmul(ps[:, 0, 0:TT * N_EXP], ones[:], rt[3][:].rearrange("p t e -> p (t e)"), start=False, stop=True)
            nc.tensor.matmul(ps[:, 1, 0:N_EXP], ones[:], rs[:, 20, :], start=True, stop=True).then_inc(rank_mm, 1)

            for c in range(2 * TT):
                pe.wait_ge(one_hots, 2 * c + 2)
                mm = nc.tensor.matmul(ps[0:CAP, 2, 0:LT], row_hot[:, c, :], tile_hot[:, c, :], start=(c == 0), stop=(c == 2 * TT - 1))
            mm.then_inc(list_mm, 1)

            def ex_transposes(e, u, src, first):
                for k in range(KT):
                    mm = nc.tensor.transpose(ps[:, k // 4, (k % 4) * COLS:(k % 4 + 1) * COLS],
                                             src[:, k * P:(k + 1) * P], ident[0:COLS, 0:COLS])
                return mm

            def gate_up(u, bank, xTu):
                for f in range(4):
                    w = (wg if f < 2 else wu)[u]
                    c0 = (f % 2) * P
                    for k in range(KT):
                        mm = nc.tensor.matmul(ps[:, bank, f * COLS:(f + 1) * COLS], w[:, k, c0:c0 + P], xTu[:, k, :],
                                              start=(k == 0), stop=(k == KT - 1))
                return mm

            def down(u, b0, hTu):
                for n in range(2):
                    for j in range(2):
                        mm = nc.tensor.matmul(ps[0:CAP, b0 + n, :], hTu[:, j, 0:CAP], wd[u][:, j, n * 512:(n + 1) * 512],
                                              start=(j == 0), stop=(j == 1))
                return mm

            def expert(it, u):
                first = isinstance(it, int)
                e = it * RING + u
                pe.wait_ge(xg_in[u % 2], 16 * (u // 2 + 1) + it * (16 * RING // 2))
                if not first or u >= 1:
                    pe.wait_ge(xT_done, e)
                ex_transposes(e, u, xg[u % 2], first).then_inc(etr_done, 1)
                if not first or u >= 1:
                    down_of(e - 1, (u - 1) % RING, (u - 1) % 2, first and u < 2, it if u else it - 1, u)
                pe.wait_ge(xT_done, e + 1)
                pe.wait_ge(wgu_in[u], it * 32 + 32)
                if not first or u >= 2:
                    pe.wait_ge(hT_done, e - 1)
                gate_up(u, 2 + u % 2, xT[u % 2]).then_inc(gu_done, 1)

            def down_of(e, slot, par, early, w_it, u):
                pe.wait_ge(hT_done, e + 1)
                pe.wait_ge(wd_in[slot], w_it * 16 + 16)
                if not early:
                    if not (isinstance(e, int) and e < 2):
                        pe.wait_ge(y_a, e - 1)
                        pe.wait_ge(y_v, e - 1)
                down(slot, 4 + 2 * par, hT[par]).then_inc(down_done, 1)

            for u in range(RING):
                expert(0, u)
            with pe.Fori(1, N_EXP // RING) as it:
                for u in range(RING):
                    expert(it, u)
            down_of(N_EXP - 1, RING - 1, 1, False, N_EXP // RING - 1, 0)

            n_ovf = pe.value_load(eid[0:1, N_OVF:N_OVF + 1], min_val=0, max_val=N_OVF)
            pe.wait_ge(xT_done, N_EXP)
            pe.wait_ge(hT_done, N_EXP)
            pe.wait_ge(y_a, N_EXP)
            pe.wait_ge(y_v, N_EXP)
            with pe.If(n_ovf > 0):
                with pe.Fori(0, N_OVF) as j:
                    with pe.If(j < n_ovf):
                        pe.wait_ge(v_x, j * 16 + 16)
                        ex_transposes(0, 0, xg[0], False).then_inc(v_tr, 1)
                        pe.wait_ge(v_xT, j + 1)
                        pe.wait_ge(v_w, j * 48 + 48)
                        gate_up(0, 2, xT[0]).then_inc(v_gu, 1)
                        pe.wait_ge(v_hT, j + 1)
                        down(0, 4, hT[0]).then_inc(down_done, 1)

        @block.scalar
        def _(act):
            def square(t):
                act.wait_ge(x_in[t % NX], 16 * (t // NX + 1))
                if t >= NX:
                    act.wait_ge(xtr_done, 2 * (t - NX + 1))
                nc.scalar.activation(xn[t % NX][:], xin[t % NX][:], ACT.Square, scale=D ** -0.5, accum_out=stat[:, 0, t:t + 1]).then_inc(sq_done, 1)

            def high(t):
                for j in range(2):
                    b = 2 * t + j
                    act.wait_ge(xtr_done, b + 1)
                    nc.scalar.copy(hThi[:, 4 * j:4 * j + 4, t * P:(t + 1) * P],
                                   ps[:, b % 4, :].rearrange("p (c q) -> p c q", c=4)).then_inc(hi_done, 1)

            def projected(i, n):
                m, g = ORDER[i], PROJ.index((i, n))
                act.wait_ge(proj_done, g + 1)
                bank = ps[:, 4 + g % 4, :]
                cols = slice(n * 512, (n + 1) * 512)
                if m in V_TILES:
                    v = V_TILES.index(m)
                    if v >= 2:
                        act.wait_ge(vtr_done, 2)
                    nc.scalar.copy(vT[v % 2][:, cols], bank).then_inc(proj_out, 1)
                elif m < 2:
                    nc.scalar.mul(qa[:, m, cols], bank, -(HD ** -0.5)).then_inc(proj_out, 1)
                elif m < 4:
                    nc.scalar.copy(ka[:, m - 2, cols], bank).then_inc(proj_out, 1)
                elif m < 10:
                    nc.scalar.mul(qb[:, m - 6, cols], bank, -(HD ** -0.5)).then_inc(proj_out, 1)
                elif m == 10:
                    for gg in range(2):
                        for side in range(2):
                            a = nc.scalar.copy(kb[side * HD:(side + 1) * HD, gg, cols], bank[gg * HD:(gg + 1) * HD, :])
                    a.then_inc(proj_out, 1)
                else:
                    nc.scalar.copy(cu[:, m - 12, PAD + n * 512:PAD + (n + 1) * 512], bank).then_inc(proj_out, 1)

            def w_high(i):
                act.wait_ge(w_in_s[0], 8 * i + 16)
                if i == 2:
                    act.wait_ge(proj_done, PROJ.index((0, 1)) + 1)
                    act.wait_ge(w_split, 4)
                nc.scalar.copy(whi[0][:], wraw[0][:]).then_inc(w_split, 1)

            for t in range(NX):
                square(t)
            for t in range(4):
                high(t)
                square(t + NX)
                if t == 1:
                    w_high(0)
            high(4)
            high(5)
            projected(0, 0)
            high(6)
            high(7)
            for i, n in PROJ[1:3]:
                projected(i, n)
            w_high(2)
            for i, n in PROJ[3:]:
                projected(i, n)

            def exponentials(u):
                s = u // 4
                act.wait_ge(bias_done, u + 1)
                buf = pbuf(u)
                if s >= NA_STEPS:
                    buf = pswa[s % 4][:, u % 4, 0:1 + steps[s][4]]
                nc.scalar.activation(buf, buf, ACT.Exp, bias=mneg[:, u:u + 1], scale=-1.0,
                                     accum_out=esum[:, u:u + 1]).then_inc(exp_done, 1)

            def o_evacuate(s):
                kind, i, g, _, _ = steps[s]
                oi = o_steps.index(s)
                act.wait_ge(pv_done, vnum[(s, last_chunk[s])] + 1)
                bank = ps[:, 6 + oi % 2, :]
                if kind == "na":
                    dst, src = oT[:, 0:2, i * P:(i + 1) * P], bank[:, 0:2 * P].rearrange("p (t q) -> p t q", t=2)
                else:
                    dst, src = oT[:, 2:6, i * P:(i + 1) * P], bank.rearrange("p (t q) -> p t q", t=4)
                nc.scalar.copy(dst, src).then_inc(o_out, 1)

            pending = []
            for u, tick in enumerate(ticks):
                if u < NU:
                    exponentials(u)
                for s in pending:
                    o_evacuate(s)
                pending = []
                for kind, s, c in tick:
                    if kind == "T" and chunk_no[(s, c)] % 2 == 1:
                        evacuate_chunk(act, nc.scalar.copy, pt_a, s, c)
                    if kind == "V" and c == last_chunk[s]:
                        pending.append(s)
            for s in pending:
                o_evacuate(s)
            for i in range(2):
                for n in range(2):
                    act.wait_ge(pool_mm, 2 * i + n + 1)
                    act.wait_ge(const_in, 16 * 9)
                    nc.scalar.mul(oT[:, 6 + i, n * 512:(n + 1) * 512], ps[:, 2 * i + n, :], pscale[:, i:i + 1]).then_inc(pool_out, 1)

            def wo_high(n, k):
                c = n * KT + k
                act.wait_ge(wo_in[c % 4], 32 * (c // 4 + 1))
                nc.scalar.copy(wohi[n][:, k, :], woraw[c % 4][:]).then_inc(wohi_done[n], 1)

            def oT_high(t):
                nc.scalar.copy(oThi[:, :, t * P:(t + 1) * P], oT[:, :, t * P:(t + 1) * P]).then_inc(oThi_done, 1)

            act.wait_ge(pool_out, 4)
            act.wait_ge(o_out, len(o_steps))
            for k in range(KT):
                wo_high(0, k)
                if k == 0:
                    oT_high(0)
            for t in range(1, TT):
                oT_high(t)

            def square2(t):
                act.wait_ge(x1_done, TT + t + 1)
                if t >= 2:
                    act.wait_ge(h2tr_done, 2 * (t - 1))
                    act.wait_ge(h2_stored[t % 2], 16 * (t // 2))
                nc.scalar.activation(h2[t % 2][:], x1[:, t, :], ACT.Square, scale=D ** -0.5, accum_out=stat[:, 2, t:t + 1]).then_inc(sq2_done, 1)

            def h2T_copy(t):
                for j in range(2):
                    act.wait_ge(h2tr_done, 2 * t + j + 1)
                    if t >= 2 and j == 0:
                        act.wait_ge(logit_mm, t - 1)
                    nc.scalar.copy(h2T[t % 2][:, 4 * j:4 * j + 4, :],
                                   ps[:, 4 + j, :].rearrange("p (c q) -> p c q", c=4)).then_inc(h2T_done, 1)

            for t in range(TT):
                square2(t)
                if t >= 1:
                    h2T_copy(t - 1)
            h2T_copy(TT - 1)
            act.wait_ge(rd, RD_GROUP)
            nc.scalar.activation(rs[:, 1, :], rs[:, 0, :], ACT.Exp).then_inc(r_exp, 1)
            act.wait_ge(rd, RD_PAIR)
            nc.scalar.activation(rs[:, 9, 0:TT], rs[:, 8, 0:TT], ACT.Exp).then_inc(r_exp, 1)

            def xT_copy(dst):
                return nc.scalar.copy(dst[:].rearrange("p (b c) q -> p b c q", b=2),
                                      ps[:, 0:2, 0:4 * COLS].rearrange("p b (c q) -> p b c q", c=4))

            def silu(dst, bank):
                return nc.scalar.activation(dst[:], ps[:, bank, 0:2 * COLS].rearrange("p (f q) -> p f q", f=2), ACT.Silu)

            def expert(it, u):
                first = isinstance(it, int)
                e = it * RING + u
                act.wait_ge(etr_done, e + 1)
                if not first or u >= 2:
                    act.wait_ge(gu_done, e - 1)
                xT_copy(xT[u % 2]).then_inc(xT_done, 1)
                if not first or u >= 1:
                    y_low(it, u)
                act.wait_ge(gu_done, e + 1)
                silu(sg[u % 2], 2 + u % 2).then_inc(silu_done, 1)

            def y_low(it, u):
                e = it * RING + u
                first = isinstance(it, int)
                par = (u - 1) % 2
                act.wait_ge(down_done, e)
                if not (first and it == 0 and u < 3):
                    act.wait_ge(y_put[par], put_count(it, u - 1))
                nc.scalar.copy(ysb[par][:, 0:512], ps[0:CAP, 4 + 2 * par, :]).then_inc(y_a, 1)

            for u in range(RING):
                expert(0, u)
            with act.Fori(1, N_EXP // RING) as it:
                for u in range(RING):
                    expert(it, u)
            y_low(N_EXP // RING, 0)

            n_ovf = act.value_load(eid[0:1, N_OVF:N_OVF + 1], min_val=0, max_val=N_OVF)
            with act.If(n_ovf > 0):
                with act.Fori(0, N_OVF) as j:
                    with act.If(j < n_ovf):
                        act.wait_ge(v_tr, j + 1)
                        xT_copy(xT[0]).then_inc(v_xT, 1)
                        act.wait_ge(v_gu, j + 1)
                        silu(sg[0], 2).then_inc(v_silu, 1)
                        act.wait_ge(down_done, j + (N_EXP + 1))
                        act.wait_ge(y_put[0], j * 16 + 16 * (N_EXP // 2))
                        nc.scalar.copy(ysb[0][:, 0:512], ps[0:CAP, 4, :]).then_inc(v_ya, 1)

            for t in range(TT):
                act.wait_ge(c_sum, 2 * (t + 1))
                nc.scalar.activation(fo[t][:], x1[:, t, :], ACT.Square, scale=D ** -0.5, accum_out=stat[:, 0, t:t + 1]).then_inc(c_sq_done, 1)

        @block.vector
        def _(dve):
            def normalise(t):
                dve.wait_ge(rstd_a, t + 1)
                dve.wait_ge(x_in[t % NX], 16 * (t // NX + 1))
                nc.vector.scalar_tensor_tensor(out=xn[t % NX][:], in0=xin[t % NX][:], scalar=stat[:, 1, t:t + 1], in1=gbc[:],
                                               op0=ALU.mult, op1=ALU.mult).then_inc(xn_done, 1)

            def low(t):
                for j in range(2):
                    b = 2 * t + j
                    dve.wait_ge(hi_done, b + 1)
                    nc.vector.tensor_tensor(hTlo[:, 4 * j:4 * j + 4, t * P:(t + 1) * P],
                                            ps[:, b % 4, :].rearrange("p (c q) -> p c q", c=4),
                                            hThi[:, 4 * j:4 * j + 4, t * P:(t + 1) * P].bitcast(F32),
                                            ALU.subtract).then_inc(lo_done, 1)

            def values(v):
                for n in range(2):
                    dve.wait_ge(vtr_done, 2 * v + n + 1)
                    nc.vector.tensor_copy(vtok[:, 4 * n:4 * n + 4, v * P:(v + 1) * P],
                                          ps[:, (2 * v + n) % 4, :].rearrange("p (c q) -> p c q", c=4)).then_inc(v_ready, 1)

            def w_low(i):
                dve.wait_ge(w_split, 2 * i + 1)
                nc.vector.tensor_tensor(wlo[0][:], wraw[0][:], whi[0][:].bitcast(F32), ALU.subtract).then_inc(w_split, 1)

            nc.vector.memset(cu[:, :, 0:PAD], 0.0).then_inc(cu_zero, 1)
            nc.vector.memset(cu[:, :, PAD + S:PAD + S + PAD], 0.0).then_inc(cu_zero, 1)
            nc.vector.memset(pwd[:], 0.0).then_inc(cu_zero, 1)
            dve.wait_ge(g_in, 16)
            normalise(0)
            normalise(1)
            for t in range(TT):
                if t + 2 < TT:
                    normalise(t + 2)
                low(t)
                if t == 1:
                    w_low(0)
            w_low(2)
            dve.wait_ge(tab_in, 16 * 3)
            dve.wait_ge(cmask_in, 32)
            dve.wait_ge(cu_zero, 3)
            nc.vector.tensor_tensor(te[:].rearrange("p h r c -> p (h r) c"),
                                    colmask[:].unsqueeze(1).to_broadcast([P, NA_HEADS * NEDGE, GRID_W]),
                                    te[:].rearrange("p h r c -> p (h r) c"), ALU.subtract).then_inc(te_ready, 1)
            dve.wait_ge(te_ready, 1)
            for h in range(NA_HEADS):
                nc.vector.tensor_tensor(ti[:, h], te[:, h, 2:2 + NINNER, :],
                                        rowmask[:].unsqueeze(2).to_broadcast([P, NINNER, GRID_W]), ALU.add).then_inc(ti_ready, 1)
            dve.wait_ge(const_in, 16 * 9)
            nc.vector.tensor_scalar(nsink[:], nsink[:], -1.0, None, ALU.mult).then_inc(sink_set, 1)
            for v in range(3):
                values(v)

            dve.wait_ge(proj_done, 2 * MT)
            dve.wait_ge(ti_ready, NA_HEADS)
            dve.wait_ge(sink_set, 1)

            def bias_and_max(u):
                s, h = u // 4, u % 4
                kind, i, g, k0, nk = steps[s]
                dve.wait_ge(score_done, u + 1)
                if kind == "na":
                    if h == 0 and s >= 3:
                        dve.wait_ge(tr_done, chunk_no[(s - 3, last_chunk[s - 3])] + 1)
                    rows = nk // GRID_W
                    r0 = k0 // GRID_W - 2 * i
                    inner = rows == 9
                    tab = ti[:, h, 0:9, :] if inner else te[:, h, r0 + 6:r0 + 6 + rows, :]
                    nc.vector.tensor_tensor_reduce(
                        out=pbuf(u).rearrange("p (b k) -> p b k", b=2), in0=ps[:, sbank(u):sbank(u) + 2, 0:nk // 2],
                        in1=tab.rearrange("p r c -> p (r c)").rearrange("p (b k) -> p b k", b=2),
                        scale=1.0, scalar=BIG, op0=ALU.add, op1=ALU.min, accum_out=mneg[:, u:u + 1]).then_inc(bias_done, 1)
                else:
                    hh = 4 * g + h
                    if h == 0:
                        before = s - 4 if s >= NA_STEPS + 4 else (5, 5, 6, 7)[s - NA_STEPS]
                        dve.wait_ge(tr_done, chunk_no[(before, last_chunk[before])] + 1)
                        nc.vector.tensor_copy(pswa[s % 4][:, :, 0], nsink[:, 4 * g:4 * g + 4]).then_inc(sink_set, 1)
                        dve.wait_ge(sink_set, 2 + s - NA_STEPS)
                    first = (k0 // P) - (i - 1)
                    nc.vector.tensor_tensor_reduce(
                        out=pbuf(u), in0=ps[:, sbank(u), 0:nk], in1=alibi[:, hh, first * P:first * P + nk],
                        scale=1.0, scalar=nsink[:, hh:hh + 1], op0=ALU.add, op1=ALU.min,
                        accum_out=mneg[:, u:u + 1]).then_inc(bias_done, 1)

            def reciprocal(u):
                dve.wait_ge(exp_done, u + 1)
                nc.vector.reciprocal(esum[:, u:u + 1], esum[:, u:u + 1]).then_inc(recip_done, 1)

            for u, tick in enumerate(ticks):
                if u < NU:
                    bias_and_max(u)
                if 0 <= u - 1 < NU:
                    reciprocal(u - 1)
                    if norm_by_vector(u - 1):
                        dve.wait_ge(recip_done, u)
                        nc.vector.tensor_scalar(pbuf(u - 1), pbuf(u - 1), esum[:, u - 1:u], None, ALU.mult).then_inc(norm_v, 1)
                for kind, s, c in tick:
                    if kind == "T" and chunk_no[(s, c)] % 2 == 0:
                        evacuate_chunk(dve, nc.vector.tensor_copy, pt_v, s, c)

            def wo_low(n, k):
                c = n * KT + k
                dve.wait_ge(wohi_done[n], k + 1)
                nc.vector.tensor_tensor(wolo[n][:, k, :], woraw[c % 4][:], wohi[n][:, k, :].bitcast(F32),
                                        ALU.subtract).then_inc(wolo_done[n], 1)

            def oT_low(t):
                dve.wait_ge(oThi_done, t + 1)
                nc.vector.tensor_tensor(oTlo[:, :, t * P:(t + 1) * P], oT[:, :, t * P:(t + 1) * P],
                                        oThi[:, :, t * P:(t + 1) * P].bitcast(F32), ALU.subtract).then_inc(oTlo_done, 1)

            for k in range(KT):
                wo_low(0, k)
                if k == 0:
                    oT_low(0)
            for t in range(1, TT):
                oT_low(t)

            def residual(g):
                n, t = g // TT, g % TT
                dve.wait_ge(out_mm, g + 1)
                dve.wait_ge(xr_in[g % 2], 16 * (g // 2 + 1))
                nc.vector.tensor_tensor(x1[:, t, n * 512:(n + 1) * 512], ps[:, g % 4, :], xres[g % 2][:], ALU.add).then_inc(x1_done, 1)

            def normalise2(t):
                dve.wait_ge(rstd_b, t + 1)
                nc.vector.scalar_tensor_tensor(out=h2[t % 2][:], in0=x1[:, t, :], scalar=stat[:, 3, t:t + 1], in1=gbc[:],
                                               op0=ALU.mult, op1=ALU.mult).then_inc(h2_done, 1)

            def take_logits(t):
                dve.wait_ge(logit_mm, t + 1)
                nc.vector.tensor_tensor(logit[:, t, :], ps[:, 6 + t % 2, 0:NR], rb[:], ALU.add).then_inc(logit_done, 1)

            dve.wait_ge(g_in, 32)
            for g in range(TT):
                residual(g)
            for t in range(TT):
                residual(TT + t)
                normalise2(t)
                if t >= 2:
                    take_logits(t - 2)
            take_logits(TT - 2)
            take_logits(TT - 1)

            count = [0]

            def step(ins):
                count[0] += 1
                ins.then_inc(rd, 1)
                dve.wait_ge(rd, count[0])

            v = nc.vector
            B8 = lambda a, n: a.unsqueeze(2).to_broadcast([P, TT, n])
            gl, el = logit[:, :, 0:N_GROUPS], logit[:, :, N_GROUPS:NR]
            w4 = misc[:, 0:4].unsqueeze(1).to_broadcast([P, TT, 4])
            w8 = misc[:, 4:12].unsqueeze(1).to_broadcast([P, TT, 8])
            iota_e = misc[:, 12:44].unsqueeze(1).to_broadcast([P, TT, N_EXP])
            iota_j = misc[:, 12:12 + N_OVF].unsqueeze(2).to_broadcast([P, N_OVF, N_EXP])
            s8 = lambda i: rs[:, i, 0:TT]
            s32 = lambda i, n: rs[:, i, 0:TT * n].rearrange("p (t n) -> p t n", t=TT)
            s64 = lambda i: rs[:, i:i + 2, :].rearrange("p a (t n) -> p (a t) n", n=8)
            dve.wait_ge(logit_done, TT)

            def first_of_best(values, best, weights, hot, top, n):
                step(v.tensor_tensor(hot, values, B8(best, n), ALU.is_ge))
                step(v.tensor_tensor(hot, hot, weights, ALU.mult))
                step(v.tensor_reduce(top, hot, AX_X, ALU.max))
                step(v.tensor_tensor(hot, hot, B8(top, n), ALU.is_equal))

            step(v.tensor_reduce(s8(2), gl, AX_X, ALU.max))
            step(v.tensor_tensor(s32(0, 4), gl, B8(s8(2), 4), ALU.subtract))
            assert count[0] == RD_GROUP
            first_of_best(gl, s8(2), w4, s32(3, 4), s8(4), 4)
            hotg = s32(3, 4).unsqueeze(3).to_broadcast([P, TT, 4, 8])
            step(v.tensor_tensor(rt[0][:].rearrange("p t (g e) -> p t g e", g=4),
                                 el.rearrange("p t (g e) -> p t g e", g=4), hotg, ALU.mult))
            step(v.tensor_reduce(s64(5), rt[0][:].rearrange("p t (g e) -> p t e g", g=4), AX_X, ALU.add))
            step(v.tensor_reduce(s8(7), s64(5), AX_X, ALU.max))
            first_of_best(s64(5), s8(7), w8, s64(10), s8(12), 8)
            step(v.scalar_tensor_tensor(out=s64(5), in0=s64(10), scalar=-BIG, in1=s64(5), op0=ALU.mult, op1=ALU.add))
            step(v.tensor_reduce(s8(13), s64(5), AX_X, ALU.max))
            step(v.tensor_tensor(s8(8), s8(13), s8(7), ALU.subtract))
            assert count[0] == RD_PAIR
            first_of_best(s64(5), s8(13), w8, s64(14), s8(12), 8)
            for k, hot in enumerate((s64(10), s64(14))):
                step(v.tensor_tensor(rt[k][:].rearrange("p t (g e) -> p t g e", g=4), hotg,
                                     hot.unsqueeze(2).to_broadcast([P, TT, 4, 8]), ALU.mult))
            step(v.tensor_tensor(rt[2][:], rt[0][:], rt[1][:], ALU.add))
            step(v.memset(rt[3][:, 0, :], 0.0))
            for t in range(1, TT):
                step(v.tensor_tensor(rt[3][:, t, :], rt[3][:, t - 1, :], rt[2][:, t - 1, :], ALU.add))
            step(v.tensor_tensor(rs[:, 20, :], rt[3][:, TT - 1, :], rt[2][:, TT - 1, :], ALU.add))
            assert count[0] == RD_COUNTED
            dve.wait_ge(r_exp, 2)
            step(v.tensor_reduce(s8(2), s32(1, 4), AX_X, ALU.add))
            step(v.reciprocal(s8(2), s8(2)))
            step(v.tensor_scalar(s8(4), s8(9), 1.0, None, ALU.add))
            step(v.reciprocal(s8(4), s8(4)))
            step(v.tensor_tensor(gates[:, 0, :], s8(2), s8(4), ALU.mult))
            step(v.tensor_tensor(gates[:, 1, :], gates[:, 0, :], s8(9), ALU.mult))
            dve.wait_ge(rank_mm, 1)
            step(v.tensor_scalar(rs[:, 16, :], ps[:, 1, 0:N_EXP], 1.0 / CAP, (CAP - 0.5) / CAP - 0.5, ALU.mult, ALU.add))
            step(v.tensor_scalar(rs[:, 16, :], rs[:, 16, :], MAGIC, None, ALU.add))
            step(v.tensor_scalar(rs[:, 16, :], rs[:, 16, :], MAGIC + 1.0, 0.0, ALU.subtract, ALU.max))
            a, b = 16, 17
            sh = 1
            while sh < N_EXP:
                step(v.tensor_copy(rs[:, b, 0:sh], rs[:, a, 0:sh]))
                step(v.tensor_tensor(rs[:, b, sh:], rs[:, a, sh:], rs[:, a, 0:N_EXP - sh], ALU.add))
                a, b = b, (18 if b == 17 else 17)
                sh *= 2
            incl = rs[:, a, :]
            step(v.tensor_tensor(rs[:, 19, :], incl, rs[:, 16, :], ALU.subtract))
            step(v.tensor_scalar(rs[:, 19, :], rs[:, 19, :], N_EXP - 1.0, None, ALU.add))
            rank = ps[:, 0, 0:TT * N_EXP].rearrange("p (t e) -> p t e", t=TT)
            step(v.tensor_scalar(rt[4][:], rank, 1.0 / CAP, 0.5 / CAP - 0.5, ALU.mult, ALU.add))
            step(v.tensor_scalar(rt[4][:], rt[4][:], MAGIC, None, ALU.add))
            step(v.tensor_scalar(rt[4][:], rt[4][:], MAGIC, None, ALU.subtract))
            step(v.scalar_tensor_tensor(out=rt[5][:], in0=rt[4][:], scalar=-float(CAP), in1=rank, op0=ALU.mult, op1=ALU.add))
            step(v.tensor_tensor(rt[6][:], rt[4][:], rs[:, 19, :].unsqueeze(1).to_broadcast([P, TT, N_EXP]), ALU.add))
            step(v.tensor_tensor(rt[6][:], rt[6][:], iota_e, ALU.subtract))
            step(v.tensor_scalar(rt[4][:], rt[4][:], 1.0, None, ALU.min))
            step(v.tensor_tensor(rt[6][:], rt[6][:], rt[4][:], ALU.mult))
            step(v.tensor_tensor(rt[6][:], rt[6][:], iota_e, ALU.add))
            step(v.scalar_tensor_tensor(out=rt[5][:], in0=rt[5][:], scalar=float(PITCH), in1=rt[6][:], op0=ALU.mult, op1=ALU.add))
            pos, row, tile = place[:, 0, :], place[:, 1, :], place[:, 2, :]
            for k in range(2):
                step(v.tensor_tensor(rt[6][:], rt[k][:], rt[5][:], ALU.mult))
                step(v.tensor_reduce(pos[:, k * TT:(k + 1) * TT], rt[6][:], AX_X, ALU.add))
            step(v.tensor_scalar(row, pos, 1.0 / PITCH, 0.5 / PITCH - 0.5, ALU.mult, ALU.add))
            step(v.tensor_scalar(row, row, MAGIC, None, ALU.add))
            step(v.tensor_scalar(row, row, MAGIC, None, ALU.subtract))
            step(v.scalar_tensor_tensor(out=tile, in0=row, scalar=-float(PITCH), in1=pos, op0=ALU.mult, op1=ALU.add))
            dve.wait_ge(h2T_done, 2 * TT)
            dve.wait_ge(logit_mm, TT)
            dve.wait_ge(out_mm, 2 * TT)
            dve.wait_ge(pc_in, 16 * 6)
            for c in range(2 * TT):
                v.tensor_scalar(row_hot[:, c, :], misc[:, 12:12 + CAP], row[:, c:c + 1], None, ALU.is_equal).then_inc(one_hots, 1)
                v.tensor_scalar(tile_hot[:, c, :], misc[:, 12:12 + LT], tile[:, c:c + 1], dvals[:, c:c + 1],
                                ALU.is_equal, ALU.mult).then_inc(one_hots, 1)
            step(v.tensor_tensor(ovf_cmp[:], iota_j, incl.unsqueeze(1).to_broadcast([P, N_OVF, N_EXP]), ALU.is_ge))
            step(v.tensor_reduce(rs[:, 21, 0:N_OVF], ovf_cmp[:], AX_X, ALU.add))
            step(v.tensor_scalar(eid[:, 0:N_OVF], rs[:, 21, 0:N_OVF], N_EXP - 1.0, None, ALU.min))
            step(v.tensor_copy(eid[:, N_OVF:N_OVF + 1], incl[:, N_EXP - 1:N_EXP]))
            dve.wait_ge(list_mm, 1)
            entry = ps[0:CAP, 2, 0:LT]
            step(v.tensor_scalar(pad[:], entry, 0.0, NOWHERE - 1.0, ALU.is_equal, ALU.mult))
            step(v.scalar_tensor_tensor(out=dest[:], in0=pad[:], scalar=-1.0, in1=entry, op0=ALU.add, op1=ALU.add))
            nc.vector.tensor_scalar(tok[:], dest[:], float(S), -float(S), ALU.is_ge, ALU.mult).then_inc(tok_done, 1)
            dve.wait_ge(tok_done, 1)
            nc.vector.tensor_tensor(tok[:], tok[:], dest[:], ALU.add).then_inc(tok_done, 1)

            def gated(sgu, dst, bank):
                return nc.vector.tensor_tensor(dst[:], sgu[:], ps[:, bank, 2 * COLS:4 * COLS].rearrange("p (f q) -> p f q", f=2), ALU.mult)

            def y_high(it, u):
                e = it * RING + u
                first = isinstance(it, int)
                par = (u - 1) % 2
                dve.wait_ge(down_done, e)
                if not (first and it == 0 and u < 3):
                    dve.wait_ge(y_put[par], put_count(it, u - 1))
                nc.vector.tensor_copy(ysb[par][:, 512:1024], ps[0:CAP, 5 + 2 * par, :]).then_inc(y_v, 1)

            def expert(it, u):
                first = isinstance(it, int)
                e = it * RING + u
                if not first or u >= 1:
                    y_high(it, u)
                dve.wait_ge(silu_done, e + 1)
                if not first or u >= 2:
                    dve.wait_ge(down_done, e - 1)
                gated(sg[u % 2], hT[u % 2], 2 + u % 2).then_inc(hT_done, 1)

            for u in range(RING):
                expert(0, u)
            with dve.Fori(1, N_EXP // RING) as it:
                for u in range(RING):
                    expert(it, u)
            y_high(N_EXP // RING, 0)

            n_ovf = dve.value_load(eid[0:1, N_OVF:N_OVF + 1], min_val=0, max_val=N_OVF)
            with dve.If(n_ovf > 0):
                with dve.Fori(0, N_OVF) as j:
                    with dve.If(j < n_ovf):
                        dve.wait_ge(v_silu, j + 1)
                        gated(sg[0], hT[0], 2).then_inc(v_hT, 1)
                        dve.wait_ge(down_done, j + (N_EXP + 1))
                        dve.wait_ge(y_put[0], j * 16 + 16 * (N_EXP // 2))
                        nc.vector.tensor_copy(ysb[0][:, 512:1024], ps[0:CAP, 5, :]).then_inc(v_yv, 1)

            def add_rows(t):
                dve.wait_ge(yc_in[t], 32)
                for k, y in enumerate((y0[t], y1[t])):
                    nc.vector.scalar_tensor_tensor(out=x1[:, t, :], in0=y[:], scalar=gates[:, k, t:t + 1], in1=x1[:, t, :],
                                                   op0=ALU.mult, op1=ALU.add).then_inc(c_sum, 1)
                    dve.wait_ge(c_sum, 2 * t + k + 1)

            def finish(t):
                dve.wait_ge(rstd_a, TT + t + 1)
                nc.vector.scalar_tensor_tensor(out=fo[t][:], in0=x1[:, t, :], scalar=stat[:, 1, t:t + 1], in1=gbc[:],
                                               op0=ALU.mult, op1=ALU.mult).then_inc(c_out, 1)

            dve.wait_ge(g_in, 48)
            add_rows(0)
            for t in range(TT):
                if t + 1 < TT:
                    add_rows(t + 1)
                finish(t)

        @block.gpsimd
        def _(pool):
            gp = nc.gpsimd

            def split(i):
                pool.wait_ge(w_in_s[i % 2], 16 * (i // 2 + 1))
                if i >= 2:
                    pool.wait_ge(proj_done, PROJ.index((i - 2, 1)) + 1)
                pool.wait_ge(w_split, 2 * i)
                gp.tensor_copy(whi[i % 2][:], wraw[i % 2][:]).then_inc(w_split, 1)
                pool.wait_ge(w_split, 2 * i + 1)
                gp.tensor_tensor(wlo[i % 2][:], wraw[i % 2][:], whi[i % 2][:].bitcast(F32), ALU.subtract).then_inc(w_split, 1)

            gp.memset(neg_half[:], -0.5).then_inc(pad_set, 1)
            pool.wait_ge(pad_set, 1)
            count = [0]

            def inverse_root(src, ready, n, done, t):
                pool.wait_ge(ready, n)
                gp.tensor_scalar(stat[:, src + 1, t:t + 1], stat[:, src, t:t + 1], EPS, None, ALU.add).then_inc(eps_added, 1)
                count[0] += 1
                pool.wait_ge(eps_added, count[0])
                gp.tensor_tensor(stat[:, src + 1, t:t + 1], stat[:, src + 1, t:t + 1], neg_half[:], ALU.pow).then_inc(done, 1)

            for t in range(TT):
                if t == 6:
                    split(1)
                inverse_root(0, sq_done, t + 1, rstd_a, t)
            pool.dma_start(colmask[:], c_colmask).then_inc(cmask_in, 16)
            pool.dma_start(rowmask[:], c_rowmask).then_inc(cmask_in, 16)
            pool.dma_start(iedge[:], c_iedge).then_inc(pc_in, 16)
            pool.dma_start(dvals[:], c_dest).then_inc(pc_in, 16)
            pool.wait_ge(cu_zero, 3)
            for g in range(4):
                half = slice((g % 2) * HD, (g % 2 + 1) * HD)
                pool.dma_start(pwd[half, g // 2, (g % 2) * HD:(g % 2 + 1) * HD], pool_w[0, g]).then_inc(pc_in, 16)
            for i in range(3, MT):
                split(i)
            pool.wait_ge(pc_in, 16 * 6)
            pool.wait_ge(proj_out, 2 * MT)
            pool.wait_ge(v_ready, 6)

            low, high, full, seq = slice(0, HD), slice(HD, P), slice(0, P), slice(PAD, PAD + S)

            def pair_sum(dst, src, rows, a, b, lo, hi):
                return lambda: gp.tensor_tensor(dst[rows, PAD + lo:PAD + hi], src[rows, PAD + lo + a:PAD + hi + a],
                                                src[rows, PAD + lo + b:PAD + hi + b], ALU.add)

            def means(i):
                c = cu[:, i, :]
                ops = [pair_sum(pa, c, full, -1, 0, -7, S + 8), pair_sum(pb, pa, full, -1, 1, -6, S + 7)]
                if i == 1:
                    ops.append(pair_sum(pa, pb, full, -2, 2, -4, S + 4))
                ops.append(lambda: gp.tensor_copy(pb[low, seq], pa[low, seq]))
                if i == 1:
                    ops.append(pair_sum(pb, pa, high, -4, 4, 0, S))
                ops.append(lambda: gp.tensor_tensor(pb[:, PAD:2 * PAD], pb[:, PAD:2 * PAD], iedge[:, i, 0:PAD], ALU.mult))
                ops.append(lambda: gp.tensor_tensor(pb[:, S:S + PAD], pb[:, S:S + PAD], iedge[:, i, PAD:2 * PAD], ALU.mult))
                ops.append(lambda: gp.tensor_scalar(pb[:, seq], pb[:, seq], iedge[:, i, 2 * PAD:2 * PAD + 1], None, ALU.mult))
                ops.append(lambda: gp.tensor_tensor(c[:, seq], pb[:, seq], c[:, seq], ALU.subtract))
                return ops

            pooling = means(0) + means(1)
            assert len(pooling) == POOL_OPS
            done = 0
            normed = 0
            for u in range(NU):
                if not norm_by_vector(u):
                    pool.wait_ge(recip_done, u + 1)
                    gp.tensor_scalar(pbuf(u), pbuf(u), esum[:, u:u + 1], None, ALU.mult).then_inc(norm_p, 1)
                    normed += 1
                if u % 5 == 4 and done < POOL_OPS:
                    pool.wait_ge(norm_p, normed)
                    pooling[done]().then_inc(pool_step, 1)
                    done += 1
                    pool.wait_ge(pool_step, done)

            pool.wait_ge(oTlo_done, TT)
            for k in range(KT):
                c = KT + k
                pool.wait_ge(wo_in[c % 4], 32 * (c // 4 + 1))
                gp.tensor_copy(wohi[1][:, k, :], woraw[c % 4][:]).then_inc(wohi_done[1], 1)
                pool.wait_ge(wohi_done[1], k + 1)
                gp.tensor_tensor(wolo[1][:, k, :], woraw[c % 4][:], wohi[1][:, k, :].bitcast(F32),
                                 ALU.subtract).then_inc(wolo_done[1], 1)

            for t in range(TT):
                inverse_root(2, sq2_done, t + 1, rstd_b, t)

            for i in range(2):
                pool.wait_ge(h2_stored[i], 16 * (TT // 2))
            pool.wait_ge(h2tr_done, 2 * TT)
            for i in range(2):
                gp.memset(xg[i][:], 0.0).then_inc(xg_zero, 1)

            pool.wait_ge(tok_done, 2)
            pool.wait_ge(xg_zero, 2)

            origin, bound_x, bound_y = (pool.alloc_register(n) for n in ("origin", "bound_x", "bound_y"))
            pool.reg_mov(origin, 0)

            def bound(reg, value):
                pool.reg_add(reg, origin, value)
                return reg

            def gather(it, u):
                first = isinstance(it, int)
                e = it * RING + u
                if not first or u >= 2:
                    pool.wait_ge(etr_done, e - 1)
                    pool.wait_ge(xg_in[u % 2], it * 32 + 16 * (u // 2))
                col = tok[:, u:u + 1] if first else tok[:, bass.ds(e, 1)]
                gp.tensor_copy(tokc[u % 2][:], col).then_inc(idx_t, 1)
                pool.wait_ge(idx_t, e + 1)
                gp.indirect_dma_start(xg[u % 2][0:CAP, :], None, h2_d, bass.IndirectOffsetOnAxis(ap=tokc[u % 2][:].bitcast(U32), axis=0),
                                      bounds_check=bound(bound_x, S - 1), oob_is_err=False).then_inc(xg_in[u % 2], 16)

            def scatter(it, u):
                f = it * RING + u - 2
                par = u % 2
                stale = isinstance(it, int) and it == 0 and u < 4
                if not stale:
                    pool.wait_ge(y_put[par], put_count(it, u - 2))
                col = dest[:, u - 2:u - 1] if isinstance(it, int) and it == 0 else dest[:, bass.ds(f, 1)]
                gp.tensor_copy(destc[par][:], col).then_inc(idx_d, 1)
                pool.wait_ge(idx_d, f + 1)
                pool.wait_ge(y_a, f + 1)
                pool.wait_ge(y_v, f + 1)
                gp.indirect_dma_start(y_d, bass.IndirectOffsetOnAxis(ap=destc[par][:].bitcast(U32), axis=0), ysb[par][:], None,
                                      bounds_check=bound(bound_y, 2 * S - 1), oob_is_err=False).then_inc(y_put[par], 16)

            for u in range(RING):
                gather(0, u)
                if u >= 2:
                    scatter(0, u)
            with pool.Fori(1, N_EXP // RING) as it:
                for u in range(RING):
                    gather(it, u)
                    scatter(it, u)
            for u in range(2):
                f = N_EXP - 2 + u
                pool.wait_ge(y_put[u], 16 * (N_EXP // 2 - 1))
                gp.tensor_copy(destc[u][:], dest[:, f:f + 1]).then_inc(idx_d, 1)
                pool.wait_ge(idx_d, f + 1)
                pool.wait_ge(y_a, f + 1)
                pool.wait_ge(y_v, f + 1)
                gp.indirect_dma_start(y_d, bass.IndirectOffsetOnAxis(ap=destc[u][:].bitcast(U32), axis=0), ysb[u][:], None,
                                      bounds_check=bound(bound_y, 2 * S - 1), oob_is_err=False).then_inc(y_put[u], 16)

            n_ovf = pool.value_load(eid[0:1, N_OVF:N_OVF + 1], min_val=0, max_val=N_OVF)
            pool.wait_ge(y_put[0], 16 * (N_EXP // 2))
            pool.wait_ge(etr_done, N_EXP)
            with pool.If(n_ovf > 0):
                with pool.Fori(0, N_OVF) as j:
                    with pool.If(j < n_ovf):
                        pool.wait_ge(y_put[0], j * 16 + 16 * (N_EXP // 2))
                        gp.tensor_copy(tokc[0][:], tok[:, bass.ds(j + N_EXP, 1)]).then_inc(v_idx, 1)
                        gp.tensor_copy(destc[0][:], dest[:, bass.ds(j + N_EXP, 1)]).then_inc(v_idx, 1)
                        pool.wait_ge(v_idx, 2 * j + 2)
                        gp.indirect_dma_start(xg[0][0:CAP, :], None, h2_d, bass.IndirectOffsetOnAxis(ap=tokc[0][:].bitcast(U32), axis=0),
                                              bounds_check=bound(bound_x, S - 1), oob_is_err=False).then_inc(v_x, 16)
                        pool.wait_ge(v_ya, j + 1)
                        pool.wait_ge(v_yv, j + 1)
                        gp.indirect_dma_start(y_d, bass.IndirectOffsetOnAxis(ap=destc[0][:].bitcast(U32), axis=0), ysb[0][:], None,
                                              bounds_check=bound(bound_y, 2 * S - 1), oob_is_err=False).then_inc(y_put[0], 16)
            for t in range(TT):
                inverse_root(0, c_sq_done, t + 1, rstd_a, t)


def constants():
    f = np.float32
    sq = np.stack([np.eye(P), np.ones((P, P)), np.triu(np.ones((P, P)), 1)]).astype(f)
    qc = np.arange(P) % GRID_W
    start = np.clip(qc - NA_COLS // 2, 0, GRID_W - NA_COLS)[:, None]
    kc = np.arange(GRID_W)[None]
    colmask = np.where((kc >= start) & (kc < start + NA_COLS), 0.0, BIG).astype(f)
    rowmask = np.zeros((P, 9), f)
    rowmask[GRID_W:, 0] = BIG
    rowmask[:GRID_W, 8] = BIG
    slopes = (2.0 ** (-8.0 * np.arange(1, SWA_HEADS + 1) / SWA_HEADS)).astype(f)
    diff = np.abs(np.arange(3 * P)[None] - np.arange(P)[:, None] - P).astype(f)
    alibi = np.where(diff[:, None] <= WINDOW, slopes[None, :, None] * diff[:, None], f(BIG)).astype(f)
    iedge = np.zeros((P, 2, 2 * PAD + 2), f)
    t = np.arange(S)
    for g, w in enumerate(POOL_WINDOWS):
        cnt = np.clip(t + w // 2, 0, S) - np.clip(t - w // 2, 0, S)
        rows = slice((g % 2) * HD, (g % 2 + 1) * HD)
        iedge[rows, g // 2, 0:PAD] = w / cnt[:PAD]
        iedge[rows, g // 2, PAD:2 * PAD] = w / cnt[-PAD:]
        iedge[rows, g // 2, 2 * PAD] = 1.0 / w
    misc = np.zeros((1, 12 + NI), f)
    misc[0, 0:4] = np.arange(4, 0, -1)
    misc[0, 4:12] = np.arange(8, 0, -1)
    misc[0, 12:] = np.arange(NI)
    k, tt = np.meshgrid(np.arange(2), np.arange(TT), indexing="ij")
    dvals = (k * S + tt * P).reshape(1, -1) + np.arange(P)[:, None] + 1
    return {"c_sq": sq, "c_colmask": colmask, "c_rowmask": rowmask, "c_alibi": alibi, "c_iedge": iedge,
            "c_misc": misc, "c_dest": dvals.astype(f)}


_INS = ["x", "norm1_g", "w_in", "nat_win", "swa_sink", "pool_w", "pool_scale", "w_out", "norm2_g",
        "router_g_w", "router_g_b", "router_e_w", "router_e_b", "expert_w_gate", "expert_w_up",
        "expert_w_down", "final_g", "c_sq", "c_colmask", "c_rowmask", "c_alibi", "c_iedge", "c_misc", "c_dest"]


def layout(inputs):
    arrays = {k: np.ascontiguousarray(v) for k, v in inputs.items()}
    edge = GRID_W - NA_COLS
    padded = np.pad(arrays.pop("nat_bias")[0], ((0, 0), (0, 0), (edge, edge)))
    arrays["nat_win"] = np.stack([padded[:, :, GRID_W - 1 - q:2 * GRID_W - 1 - q] for q in range(GRID_W)])
    arrays.update(constants())
    return arrays


def kernel(**inputs):
    import concourse.bacc as bacc
    from concourse.bass_utils import run_bass_kernel_spmd

    nc = bacc.Bacc("TRN2", target_bir_lowering=False, num_devices=1)
    arrays = layout(inputs)
    args = [nc.dram_tensor(f"in_{n}", arrays[n].shape, mybir.dt.from_np(arrays[n].dtype), kind="ExternalInput").ap()
            for n in _INS]
    args.append(nc.dram_tensor("out_0", (1, S, D), F32, kind="ExternalOutput").ap())
    encoder(nc, *args)
    r = run_bass_kernel_spmd(nc, [{f"in_{n}": arrays[n] for n in _INS}], core_ids=[0])
    return r.results[0]["out_0"]
```

```python
from contextlib import ExitStack

import numpy as np

import concourse.bass as bass
from concourse import mybir

ALU = mybir.AluOpType
ACT = mybir.ActivationFunctionType
F32 = mybir.dt.float32
F32R = mybir.dt.float32r
I32 = mybir.dt.int32
U32 = mybir.dt.uint32
AX_X = mybir.AxisListType.X

P = 128
D = 1024
S = 1024
TT = S // P
KT = D // P
HD = 64
GRID_W = 64
ROWS = S // GRID_W
NA_HEADS, NA_ROWS, NA_COLS = 4, 8, 16
SWA_HEADS, SWA_KV, WINDOW = 8, 2, 128
POOL_WINDOWS = (2, 4, 8, 16)
PAD = 8
D_IN = 3 * NA_HEADS * HD + SWA_HEADS * HD + 2 * SWA_KV * HD + len(POOL_WINDOWS) * HD
MT = D_IN // P
N_GROUPS, PER_GROUP, N_EXP, DE = 4, 8, 32, 256
NR = N_GROUPS + N_EXP
EPS = 1e-6
BIG = 1e30
CAP = 80
COLS = 96
N_OVF = (2 * S) // (CAP + 1)
PITCH = 64
NI = 96
LT = N_EXP + N_OVF
NOWHERE = 4096
RING = 4
MAGIC = 12582912.0

MIX_FROM = 8
KLO_AT = 33
SPLIT_AHEAD = 6
POOL_LAG = 2
POOL_OPS = 16
RD_GROUP, RD_PAIR, RD_COUNTED = 2, 16, 32

ORDER = [4, 0, 5, 1, 11, 12, 13, 2, 3, 10, 6, 7, 8, 9]
V_TILES = [4, 5, 11]
PROJ = [(0, 0), (1, 0), (0, 1), (1, 1)] + [(i, n) for i in range(2, 14) for n in range(2)]
NX = 4


def na_rows(i):
    lo = min(max(2 * i - NA_ROWS // 2, 0), ROWS - NA_ROWS)
    hi = min(max(2 * i + 1 - NA_ROWS // 2, 0), ROWS - NA_ROWS) + NA_ROWS
    return lo, hi - lo


def attention_plan():
    steps = []
    for i in range(TT):
        lo, n = na_rows(i)
        steps.append(("na", i, 0, lo * GRID_W, n * GRID_W))
    for b in range(TT):
        lo, hi = max(b - 1, 0), min(b + 2, TT)
        for g in range(SWA_KV):
            steps.append(("swa", b, g, lo * P, (hi - lo) * P))
    lag = 4
    ticks = [[] for _ in range(4 * len(steps) + lag + 4)]
    late = []
    for s, (kind, i, g, k0, nk) in enumerate(steps):
        nc_ = -(-nk // P)
        items = []
        for c in range(nc_):
            items.append(("T", s, c))
            items += late
            late = [("V", s, c)] if kind == "na" or g == 1 else []
        if s == len(steps) - 1:
            items += late
        for j, it in enumerate(items):
            ticks[4 * s + 3 + lag + (4 * j) // len(items)].append(it)
    return steps, ticks


def encoder(nc, x, norm1_g, w_in, nat_win, swa_sink, pool_w, pool_scale, w_out, norm2_g,
            rg_w, rg_b, re_w, re_b, e_gate, e_up, e_down, final_g,
            c_sq, c_colmask, c_rowmask, c_alibi, c_iedge, c_misc, c_dest, out):
    steps, ticks = attention_plan()
    NU = 4 * len(steps)

    h2_d = nc.dram_tensor("h2_rows", [S, D], F32).ap()
    y_d = nc.dram_tensor("expert_rows", [2 * S, D], F32).ap()

    with ExitStack() as ctx:
        KB = 1024
        arena = ctx.enter_context(nc.sbuf_tensor("arena", [P, 203 * 256 + 160], F32))
        base = nc.sbuf_base - (203 * KB + 640)
        del arena

        def at(name, shape, dt, off):
            return nc.alloc_sbuf_tensor_at(name, shape, dt, offset=base + int(off))

        def sem(name):
            return ctx.enter_context(nc.semaphore(name))

        o = 0
        ident = at("ident", [P, P], F32, o); o += 512
        ones = at("ones", [P, P], F32, o); o += 512
        ut = at("ut", [P, P], F32, o); o += 512
        gbc = at("gbc", [P, D], F32, o); o += 4096
        rw = at("rw", [P, KT, NR], F32, o); o += KT * NR * 4
        rb = at("rb", [P, NR], F32, o); o += 160
        misc = at("misc", [P, 12 + NI], F32, o); o += 448
        nsink = at("nsink", [P, SWA_HEADS], F32, o); o += 32
        pscale = at("pscale", [P, 2], F32, o); o += 32
        stat = at("stat", [P, 4, TT], F32, o); o += 128
        mneg = at("mneg", [P, NU], F32, o); o += 4 * NU
        esum = at("esum", [P, NU], F32, o); o += 4 * NU
        logit = at("logit", [P, TT, NR], F32, o); o += TT * NR * 4
        gates = at("gates", [P, 2, TT], F32, o); o += 64
        pwd = at("pwd", [P, 2, P], F32, o); o += 1024
        colmask = at("colmask", [P, GRID_W], F32, o); o += 256
        rowmask = at("rowmask", [P, 9], F32, o); o += 64
        iedge = at("iedge", [P, 2, 2 * PAD + 2], F32, o); o += 160
        dvals = at("dvals", [P, 2 * TT], F32, o); o += 64
        neg_half = at("neg_half", [P, 1], F32, o); o += 32
        PERSIST = 11 * KB + 128
        assert o <= PERSIST, o
        TD, H, W, Q, V, CU, TMP = PERSIST, 47 * KB, 111 * KB, 135 * KB, 175 * KB, 187 * KB, 195 * KB + 256
        xin = [at(f"xin{i}", [P, D], F32, TD + 4096 * i) for i in range(NX)]
        xn = [at(f"xn{i}", [P, D], F32, TD + 4096 * (NX + i)) for i in range(NX)]
        hThi = at("hThi", [P, KT, S], F32R, H)
        hTlo = at("hTlo", [P, KT, S], F32R, H + 32 * KB)
        wraw = [at(f"wraw{i}", [P, KT, P], F32, W + 4096 * i) for i in range(2)]
        whi = [at(f"whi{i}", [P, KT, P], F32R, W + 8192 + 4096 * i) for i in range(2)]
        wlo = [at(f"wlo{i}", [P, KT, P], F32R, W + 16384 + 4096 * i) for i in range(2)]
        qa = at("qa", [P, 2, S], F32, Q)
        ka = at("ka", [P, 2, S], F32, Q + 8 * KB)
        qb = at("qb", [P, 4, S], F32, Q + 16 * KB)
        kb = at("kb", [P, 2, S], F32, Q + 32 * KB)
        vtok = at("vtok", [P, TT, 3 * P], F32, V)
        cu = at("cu", [P, 2, S + 2 * PAD], F32, CU)
        vT = [at(f"vT{i}", [P, S], F32, TMP + 4096 * i) for i in range(2)]
        NEDGE, NINNER = 14, 9
        te = at("te", [P, NA_HEADS, NEDGE, GRID_W], F32, TD)
        ti = at("ti", [P, NA_HEADS, NINNER, GRID_W], F32, TD + NA_HEADS * NEDGE * GRID_W * 4)
        alibi = at("alibi", [P, SWA_HEADS, 3 * P], F32, TD + NA_HEADS * (NEDGE + NINNER) * GRID_W * 4)
        oT = at("oT", [P, KT, S], F32, H)
        pna = [at(f"pna{i}", [P, 4, 9 * GRID_W], F32, H + 32 * KB + i * 9216) for i in range(3)]
        pswa = [at(f"pswa{i}", [P, 4, 3 * P + 1], F32, H + 32 * KB + off) for i, off in enumerate((18432, 24608, 0, 9216))]
        ptna = [at(f"ptna{i}", [P, 5, 512], F32, W + i * 10 * KB) for i in range(2)]
        ptswa = [at(f"ptswa{i}", [P, 3, 2, 512], F32, W + i * 12 * KB) for i in range(2)]
        khi = at("khi", [P, 2, S], F32R, TD)
        klo = at("klo", [P, 2, S], F32R, Q + 8 * KB)
        qs = [at(f"qs{i}", [P, SWA_HEADS, P], F32R, (TD + 8 * KB, Q)[i]) for i in range(2)]
        pa = at("pa", [P, S + 2 * PAD], F32, TMP)
        pb = at("pb", [P, S + 2 * PAD], F32, TMP + 4160)
        oThi = at("oThi", [P, KT, S], F32R, W)
        oTlo = at("oTlo", [P, KT, S], F32R, W + 32 * KB)
        wohi = [at(f"wohi{n}", [P, KT, 512], F32R, H + 32 * KB * (1 - n)) for n in range(2)]
        wolo = [at(f"wolo{n}", [P, KT, 512], F32R, H + 32 * KB * (1 - n) + 16 * KB) for n in range(2)]
        woraw = [at(f"woraw{i}", [P, 512], F32, TD + 15 * KB + 2048 * i if i < 4 else V + 2048 * (i - 4)) for i in range(8)]
        xres = [at(f"xres{i}", [P, 512], F32, V + 8192 + 2048 * i) for i in range(2)]
        x1 = at("x1", [P, TT, D], F32, TD)
        h2 = [at(f"h2{i}", [P, D], F32, CU + 4096 * i) for i in range(2)]
        h2T = [at(f"h2T{i}", [P, KT, P], F32, TMP + 4096 * i) for i in range(2)]
        rt = [at(f"rt{i}", [P, TT, N_EXP], F32, V + 1024 * i) for i in range(8)]
        rs = at("rs", [P, 24, 32], F32, V + 8192)
        place = at("place", [P, 3, 2 * TT], F32, V + 8192 + 3072)
        row_hot = at("row_hot", [P, 2 * TT, CAP], F32, TMP)
        tile_hot = at("tile_hot", [P, 2 * TT, LT], F32, H + 24 * KB)
        eoff = [H + 32 * KB, W, W + 24 * KB, H]
        wg = [at(f"wg{i}", [P, KT, DE], F32, eoff[i]) for i in range(RING)]
        wu = [at(f"wu{i}", [P, KT, DE], F32, eoff[i] + 8 * KB) for i in range(RING)]
        wd = [at(f"wd{i}", [P, 2, D], F32, eoff[i] + 16 * KB) for i in range(RING)]
        pad = at("pad", [CAP, LT], F32, V + 8192 + 3072 + 256)
        wdhi = [at(f"wdhi{i}", [P, 2, D], F32R, (H + 24 * KB, V)[i]) for i in range(2)]
        wdlo = [at(f"wdlo{i}", [P, 2, D], F32R, eoff[i] + 16 * KB) for i in range(RING)]
        dest = at("dest", [CAP, LT], I32, W + 48 * KB)
        tok = at("tok", [CAP, LT], I32, W + 48 * KB + 256)
        tokc = [at(f"tokc{i}", [CAP, 1], I32, W + 48 * KB + 704 + 32 * i) for i in range(2)]
        destc = [at(f"destc{i}", [CAP, 1], I32, W + 48 * KB + 768 + 32 * i) for i in range(2)]
        ovf_cmp = at("ovf_cmp", [P, N_OVF, N_EXP], F32, H + 28 * KB)
        eid = at("eid", [P, 32], I32, W + 48 * KB + 576)
        sg = [at(f"sg{i}", [P, 2, COLS], F32, W + 49 * KB + 768 * i) for i in range(2)]
        hT = [at(f"hT{i}", [P, 2, COLS], F32, W + 51 * KB + 768 * i) for i in range(2)]
        hThi_e = [at(f"hThi_e{i}", [P, 2, CAP], F32R, V + 8 * KB + 640 * i) for i in range(2)]
        hTlo_e = [at(f"hTlo_e{i}", [P, 2, CAP], F32R, V + 8 * KB + 1280 + 640 * i) for i in range(2)]
        ysb = [at(f"ysb{i}", [CAP, D], F32, W + 53 * KB + 4096 * i) for i in range(2)]
        xg = [at(f"xg{i}", [COLS, D], F32, CU + 4096 * i) for i in range(2)]
        xT = [at(f"xT{i}", [P, KT, COLS], F32, TMP + 3072 * i) for i in range(2)]
        y0 = [at(f"y0{i}", [P, D], F32, H + 8192 * i) for i in range(TT)]
        y1 = [at(f"y1{i}", [P, D], F32, H + 8192 * i + 4096) for i in range(TT)]
        fo = [at(f"fo{i}", [P, D], F32, W + 4096 * i) for i in range(TT)]

        ps = ctx.enter_context(nc.psum_tensor("ps", [P, 8, 512], F32))

        const_in = sem("const_in")
        mats_in = sem("mats_in")
        g_in = sem("g_in")
        x_in = [sem(f"x_in{i}") for i in range(NX)]
        sq_done = sem("sq_done")
        eps_added = sem("eps_added")
        rstd_a = sem("rstd_a")
        xn_done = sem("xn_done")
        xtr_done = sem("xtr_done")
        hi_done = sem("hi_done")
        lo_done = sem("lo_done")
        w_in_s = [sem(f"w_in{i}") for i in range(2)]
        w_split = sem("w_split")
        proj_done = sem("proj_done")
        proj_out = sem("proj_out")
        vtr_done = sem("vtr_done")
        v_ready = sem("v_ready")
        cu_zero = sem("cu_zero")
        tab_in = sem("tab_in")
        cmask_in = sem("cmask_in")
        pc_in = sem("pc_in")
        idx_t = sem("idx_t")
        idx_d = sem("idx_d")
        te_ready = sem("te_ready")
        ti_ready = sem("ti_ready")
        sink_set = sem("sink_set")
        khi_done = sem("khi_done")
        klo_done = sem("klo_done")
        qhi_done = sem("qhi_done")
        qlo_done = sem("qlo_done")
        score_done = sem("score_done")
        bias_done = sem("bias_done")
        exp_done = sem("exp_done")
        recip_done = sem("recip_done")
        norm_p = sem("norm_p")
        norm_v = sem("norm_v")
        tr_done = sem("tr_done")
        pt_v = sem("pt_v")
        pt_a = sem("pt_a")
        pv_done = sem("pv_done")
        o_out = sem("o_out")
        pool_step = sem("pool_step")
        pool_mm = sem("pool_mm")
        pool_out = sem("pool_out")
        oThi_done = sem("oThi_done")
        oTlo_done = sem("oTlo_done")
        wo_in = [sem(f"wo_in{i}") for i in range(8)]
        wohi_done = [sem(f"wohi_done{n}") for n in range(2)]
        wolo_done = [sem(f"wolo_done{n}") for n in range(2)]
        xr_in = [sem(f"xr_in{i}") for i in range(2)]
        out_mm = sem("out_mm")
        x1_done = sem("x1_done")
        sq2_done = sem("sq2_done")
        rstd_b = sem("rstd_b")
        h2_done = sem("h2_done")
        h2_stored = [sem(f"h2_stored{i}") for i in range(2)]
        h2tr_done = sem("h2tr_done")
        h2T_done = sem("h2T_done")
        logit_mm = sem("logit_mm")
        logit_done = sem("logit_done")
        rd = sem("rd")
        r_exp = sem("r_exp")
        rank_mm = sem("rank_mm")
        pad_set = sem("pad_set")
        one_hots = sem("one_hots")
        list_mm = sem("list_mm")
        tok_done = sem("tok_done")
        wgu_in = [sem(f"wgu_in{i}") for i in range(RING)]
        wd_in = [sem(f"wd_in{i}") for i in range(RING)]
        xg_zero = sem("xg_zero")
        xg_in = [sem(f"xg_in{i}") for i in range(2)]
        etr_done = sem("etr_done")
        xT_done = sem("xT_done")
        gu_done = sem("gu_done")
        silu_done = sem("silu_done")
        hT_done = sem("hT_done")
        h_made = sem("h_made")
        hTlo_done = sem("hTlo_done")
        wdhi_done = sem("wdhi_done")
        wdlo_done = sem("wdlo_done")
        down_done = sem("down_done")
        y_a = sem("y_a")
        y_v = sem("y_v")
        y_put = [sem(f"y_put{i}") for i in range(2)]
        v_w = sem("v_w")
        v_idx = sem("v_idx")
        v_x = sem("v_x")
        v_tr = sem("v_tr")
        v_xT = sem("v_xT")
        v_gu = sem("v_gu")
        v_silu = sem("v_silu")
        v_hT = sem("v_hT")
        v_ya = sem("v_ya")
        v_yv = sem("v_yv")
        yc_in = [sem(f"yc_in{i}") for i in range(TT)]
        c_sum = sem("c_sum")
        c_sq_done = sem("c_sq_done")
        c_out = sem("c_out")
        out_put = sem("out_put")

        block = ctx.enter_context(nc.Block())

        chunk_no = {}
        vnum = {}
        for tick in ticks:
            for kind, s, c in tick:
                if kind == "T":
                    chunk_no[(s, c)] = len(chunk_no)
                else:
                    vnum[(s, c)] = len(vnum)
        last_chunk = {s: max(c for (s_, c) in chunk_no if s_ == s) for s in range(len(steps))}
        NA_STEPS = TT
        o_steps = [s for s in range(len(steps)) if steps[s][0] == "na" or steps[s][2] == 1]

        na_chunks = sum(s < NA_STEPS for s, _ in chunk_no)

        def by_vector(n):
            return n % 2 == 0 if n < na_chunks else n % 3 == 0

        def chunk_ready(eng, n):
            if n >= 0:
                mine = by_vector(n)
                eng.wait_ge(pt_v if mine else pt_a, sum(by_vector(m) == mine for m in range(n + 1)))

        def norm_by_vector(u):
            return u % 2 == 1 if u < 4 * NA_STEPS else u % 8 in (3, 6)

        def split_block(u):
            b, r = divmod(u - 4 * NA_STEPS + SPLIT_AHEAD, 8)
            return (b, r) if r < 2 and 1 <= b < TT else (None, None)

        def wo_buf(c):
            return c if c < 4 else 4 + c % 4

        def pbuf(u):
            s = u // 4
            if s < NA_STEPS:
                return pna[s % 3][:, u % 4, 0:steps[s][4]]
            return pswa[s % 4][:, u % 4, 1:1 + steps[s][4]]

        def sbank(u):
            return 2 * (u % 2) if u // 4 < NA_STEPS else u % 4

        def put_count(it, v):
            return it * (16 * RING // 2) + 16 * ((v - 2) // 2 + 1)

        def evacuate_chunk(eng, copy, done, s, c):
            n = chunk_no[(s, c)]
            kind, i, g, k0, nk = steps[s]
            w = min(P, nk - c * P)
            eng.wait_ge(tr_done, n + 1)
            if kind == "na":
                if s >= 2:
                    eng.wait_ge(pv_done, vnum[(s - 2, last_chunk[s - 2])] + 1)
                copy(ptna[s % 2][0:w, c, :], ps[0:w, 4 + n % 2, :]).then_inc(done, 1)
            else:
                before = NA_STEPS - 1 if i < 2 else NA_STEPS + 2 * (i - 2) + 1
                eng.wait_ge(pv_done, vnum[(before, last_chunk[before])] + 1)
                copy(ptswa[i % 2][:, c, g, :], ps[:, 4 + n % 2, :]).then_inc(done, 1)

        @block.sync
        def _(sp):
            def load_x(t):
                if t >= NX:
                    sp.wait_ge(xn_done, t - NX + 1)
                sp.dma_start(xin[t % NX][:], x[0, t * P:(t + 1) * P, :]).then_inc(x_in[t % NX], 16)

            def load_w(i):
                m = ORDER[i]
                if i >= 2:
                    sp.wait_ge(w_split, 2 * (i - 1))
                sp.dma_start(wraw[i % 2][:], w_in[0, :, m * P:(m + 1) * P].rearrange("(k p) n -> p k n", p=P)
                             ).then_inc(w_in_s[i % 2], 16)

            load_x(0)
            sp.dma_start(gbc[:], norm1_g.partition_broadcast(P)).then_inc(g_in, 16)
            sp.dma_start(ident[:], c_sq[0]).then_inc(mats_in, 16)
            load_x(1)
            load_w(0)
            for t in range(2, NX):
                load_x(t)
            load_w(1)
            for t in range(NX, TT):
                load_x(t)
            sp.dma_start(ones[:], c_sq[1]).then_inc(const_in, 16)
            sp.dma_start(ut[:], c_sq[2]).then_inc(const_in, 16)
            sp.dma_start(misc[:], c_misc.partition_broadcast(P)).then_inc(const_in, 16)
            sp.dma_start(rb[:, 0:N_GROUPS], rg_b.partition_broadcast(P)).then_inc(const_in, 16)
            sp.dma_start(rb[:, N_GROUPS:NR], re_b.partition_broadcast(P)).then_inc(const_in, 16)
            sp.dma_start(rw[:, :, 0:N_GROUPS], rg_w[0].rearrange("(k p) n -> p k n", p=P)).then_inc(const_in, 16)
            sp.dma_start(rw[:, :, N_GROUPS:NR], re_w[0].rearrange("(k p) n -> p k n", p=P)).then_inc(const_in, 16)
            sp.dma_start(nsink[:], swa_sink.partition_broadcast(P)).then_inc(const_in, 16)
            with nc.allow_non_contiguous_dma(reason="256 scales"):
                sp.dma_start(pscale[:], pool_scale[0].rearrange("(i p) -> p i", p=P)).then_inc(const_in, 16)
            sp.wait_ge(xtr_done, 2 * TT)
            for a in range(2):
                sp.dma_start(te[a * GRID_W:(a + 1) * GRID_W], nat_win[:, :, 1 - a:1 - a + NEDGE, :]).then_inc(tab_in, 16)
            sp.dma_start(alibi[:], c_alibi).then_inc(tab_in, 16)
            for i in range(2, MT):
                load_w(i)
            sp.dma_start(gbc[:], norm2_g.partition_broadcast(P)).then_inc(g_in, 16)

            def load_wo(n, k):
                c = n * KT + k
                if c >= 8:
                    sp.wait_ge(wolo_done[(c - 4) // KT], (c - 4) % KT + 1)
                cols = slice(n * 512, (n + 1) * 512)
                dst = woraw[wo_buf(c)]
                if 2 <= k < 6:
                    for g in range(2):
                        r0 = 256 + (4 * g + k - 2) * HD
                        sp.dma_start(dst[g * HD:(g + 1) * HD, :], w_out[0, r0:r0 + HD, cols]).then_inc(wo_in[wo_buf(c)], 16)
                else:
                    sp.dma_start(dst[:], w_out[0, k * P:(k + 1) * P, cols]).then_inc(wo_in[wo_buf(c)], 32)

            def load_xres(g):
                n, t = g // TT, g % TT
                if g >= 2:
                    sp.wait_ge(x1_done, g - 1)
                sp.dma_start(xres[g % 2][:], x[0, t * P:(t + 1) * P, n * 512:(n + 1) * 512]).then_inc(xr_in[g % 2], 16)

            sp.wait_ge(bias_done, 4 * NA_STEPS)
            for k in range(4):
                load_wo(0, k)
            sp.wait_ge(o_out, len(o_steps))
            for k in range(4, KT):
                load_wo(0, k)
            load_xres(0)
            load_xres(1)
            for k in range(4):
                load_wo(1, k)
            for g in range(2, 8):
                load_xres(g)
                if g < 6:
                    load_wo(1, g + 2)

            def load_expert(e, u, dynamic):
                g_src = e_gate[0, e] if not dynamic else e_gate[0, bass.ds(e, 1)].rearrange("a d f -> (a d) f")
                u_src = e_up[0, e] if not dynamic else e_up[0, bass.ds(e, 1)].rearrange("a d f -> (a d) f")
                d_src = e_down[0, e] if not dynamic else e_down[0, bass.ds(e, 1)].rearrange("a d f -> (a d) f")
                return (g_src.rearrange("(k p) f -> p k f", p=P), u_src.rearrange("(k p) f -> p k f", p=P),
                        d_src.rearrange("(k p) f -> p k f", p=P))

            def fetch_expert(e, u, dynamic=False):
                a, b, c = load_expert(e, u, dynamic)
                if dynamic:
                    sp.wait_ge(gu_done, e - (RING - 1))
                sp.dma_start(wg[u][:], a).then_inc(wgu_in[u], 16)
                sp.dma_start(wu[u][:], b).then_inc(wgu_in[u], 16)
                if dynamic:
                    sp.wait_ge(down_done, e - (RING - 1))
                sp.dma_start(wd[u][:], c).then_inc(wd_in[u], 16)

            def store_h2(t):
                sp.wait_ge(h2_done, t + 1)
                sp.dma_start(h2_d[t * P:(t + 1) * P, :], h2[t % 2][:]).then_inc(h2_stored[t % 2], 16)

            sp.wait_ge(out_mm, TT)
            fetch_expert(0, 0)
            for g in range(8, 2 * TT):
                load_xres(g)
                if g >= 10:
                    store_h2(g - 10)
            store_h2(TT - 2)
            store_h2(TT - 1)
            sp.wait_ge(out_mm, 2 * TT)
            for u in range(1, RING):
                fetch_expert(u, u)
            with sp.Fori(1, N_EXP // RING) as it:
                for u in range(RING):
                    fetch_expert(it * RING + u, u, True)
            sp.dma_start(gbc[:], final_g.rearrange("(a d) -> a d", a=1).partition_broadcast(P)).then_inc(g_in, 16)
            sp.wait_ge(down_done, N_EXP)
            n_ovf = sp.value_load(eid[0:1, N_OVF:N_OVF + 1], min_val=0, max_val=N_OVF)
            with sp.If(n_ovf > 0):
                with sp.Fori(0, N_OVF) as j:
                    with sp.If(j < n_ovf):
                        e = sp.value_load(eid[0:1, bass.ds(j, 1)], min_val=0, max_val=N_EXP - 1)
                        a, b, c = load_expert(e, 0, True)
                        sp.wait_ge(down_done, j + N_EXP)
                        sp.dma_start(wg[0][:], a).then_inc(v_w, 16)
                        sp.dma_start(wu[0][:], b).then_inc(v_w, 16)
                        sp.dma_start(wd[0][:], c).then_inc(v_w, 16)

            sp.wait_ge(y_put[1], 16 * (N_EXP // 2))
            sp.wait_ge(y_put[0], n_ovf * 16 + 16 * (N_EXP // 2))

            def load_rows(t):
                sp.dma_start(y0[t][:], y_d[t * P:(t + 1) * P, :]).then_inc(yc_in[t], 16)
                sp.dma_start(y1[t][:], y_d[S + t * P:S + (t + 1) * P, :]).then_inc(yc_in[t], 16)

            def store(t):
                sp.wait_ge(c_out, t + 1)
                sp.dma_start(out[0, t * P:(t + 1) * P, :], fo[t][:]).then_inc(out_put, 16)

            for t in range(TT):
                load_rows(t)
            for t in range(TT):
                store(t)
            sp.wait_ge(out_put, 16 * TT)

        @block.tensor
        def _(pe):
            def x_transposes(t):
                pe.wait_ge(xn_done, t + 1)
                for j in range(2):
                    b = 2 * t + j
                    if b >= 4:
                        pe.wait_ge(lo_done, b - 3)
                    for c in range(4):
                        k = 4 * j + c
                        mm = nc.tensor.transpose(ps[:, b % 4, c * P:(c + 1) * P], xn[t % NX][:, k * P:(k + 1) * P], ident[:])
                    mm.then_inc(xtr_done, 1)

            def project(i, n):
                g = PROJ.index((i, n))
                pe.wait_ge(w_split, 2 * (i + 1))
                pe.wait_ge(lo_done, 8 * (n + 1))
                if g >= 4:
                    pe.wait_ge(proj_out, g - 3)
                bank = ps[:, 4 + g % 4, :]
                cols = slice(n * 512, (n + 1) * 512)
                for k in range(KT):
                    nc.tensor.matmul(bank, whi[i % 2][:, k, :], hThi[:, k, cols], start=(k == 0), stop=False)
                    nc.tensor.matmul(bank, whi[i % 2][:, k, :], hTlo[:, k, cols], start=False, stop=False)
                    mm = nc.tensor.matmul(bank, wlo[i % 2][:, k, :], hThi[:, k, cols], start=False, stop=(k == KT - 1))
                mm.then_inc(proj_done, 1)

            def v_transposes(v):
                pe.wait_ge(proj_out, PROJ.index((2 * v, 1)) + 1)
                for n in range(2):
                    b = 2 * v + n
                    if b >= 4:
                        pe.wait_ge(v_ready, b - 3)
                    for c in range(4):
                        mm = nc.tensor.transpose(ps[:, b % 4, c * P:(c + 1) * P],
                                                 vT[v % 2][:, (4 * n + c) * P:(4 * n + c + 1) * P], ident[:])
                    mm.then_inc(vtr_done, 1)

            pe.wait_ge(mats_in, 16)
            for t in range(4):
                x_transposes(t)
            project(0, 0)
            x_transposes(4)
            x_transposes(5)
            project(1, 0)
            x_transposes(6)
            x_transposes(7)
            for i, n in PROJ[2:]:
                project(i, n)
                if n == 1 and i in (1, 3, 5):
                    v_transposes(i // 2)

            def scores(u):
                s, h = u // 4, u % 4
                kind, i, g, k0, nk = steps[s]
                if s < NA_STEPS:
                    if u >= 2:
                        pe.wait_ge(bias_done, u - 1)
                    q = qa[(h % 2) * HD:(h % 2 + 1) * HD, h // 2, i * P:(i + 1) * P]
                    half = nk // 2
                    for r in range(2):
                        k = ka[(h % 2) * HD:(h % 2 + 1) * HD, h // 2, k0 + r * half:k0 + (r + 1) * half]
                        mm = nc.tensor.matmul(ps[:, sbank(u) + r, 0:half], q, k, start=True, stop=True)
                else:
                    pe.wait_ge(bias_done, max(u - 3, 4 * NA_STEPS))
                    hh = 4 * g + h
                    side = slice((hh % 2) * HD, (hh % 2 + 1) * HD)
                    if i == 0:
                        mm = nc.tensor.matmul(ps[:, sbank(u), 0:nk], qb[side, hh // 2, i * P:(i + 1) * P],
                                              kb[side, g, k0:k0 + nk], start=True, stop=True)
                    else:
                        if hh == 0:
                            pe.wait_ge(klo_done, SWA_KV)
                            pe.wait_ge(qlo_done, 2 * i)
                        nc.tensor.matmul(ps[:, sbank(u), 0:nk], qs[i % 2][:, hh, :], khi[:, g, k0:k0 + nk], start=True, stop=False)
                        mm = nc.tensor.matmul(ps[:, sbank(u), 0:nk], qs[i % 2][:, hh, :], klo[:, g, k0:k0 + nk], start=False, stop=True)
                mm.then_inc(score_done, 1)

            def transposes(s, c):
                n = chunk_no[(s, c)]
                w = min(P, steps[s][4] - c * P)
                if c == 0:
                    pe.wait_ge(norm_p, sum(not norm_by_vector(u) for u in range(4 * s + 4)))
                    pe.wait_ge(norm_v, sum(norm_by_vector(u) for u in range(4 * s + 4)))
                chunk_ready(pe, n - 2)
                for h in range(4):
                    mm = nc.tensor.transpose(ps[0:w, 4 + n % 2, h * P:(h + 1) * P],
                                             pbuf(4 * s + h)[:, c * P:c * P + w], ident[:])
                mm.then_inc(tr_done, 1)

            def times_values(s, c):
                kind, i, g, k0, nk = steps[s]
                oi = o_steps.index(s)
                w = min(P, nk - c * P)
                tile = k0 // P + c
                chunk_ready(pe, chunk_no[(s, c)])
                if c == 0 and oi >= 2:
                    pe.wait_ge(o_out, oi - 1)
                bank = ps[:, 6 + oi % 2, :]
                if kind == "na":
                    for h in range(4):
                        half = slice((h % 2) * HD, (h % 2 + 1) * HD)
                        mm = nc.tensor.matmul(bank[half, (h // 2) * P:(h // 2 + 1) * P],
                                              vtok[0:w, tile, h * HD:(h + 1) * HD], ptna[s % 2][0:w, c, h * P:(h + 1) * P],
                                              start=(c == 0 and h < 2), stop=(c == last_chunk[s]), skip_group_check=True)
                else:
                    chunk_ready(pe, chunk_no[(s - 1, c)])
                    for gg in range(2):
                        mm = nc.tensor.matmul(bank[gg * HD:(gg + 1) * HD, :], vtok[:, tile, 256 + gg * HD:256 + (gg + 1) * HD],
                                              ptswa[i % 2][:, c, gg, :], start=(c == 0), stop=(c == last_chunk[s]))
                mm.then_inc(pv_done, 1)

            def pooled(i, n):
                pe.wait_ge(pool_step, POOL_OPS)
                mm = nc.tensor.matmul(ps[:, 2 * i + n, :], pwd[:, i, :], cu[:, i, PAD + n * 512:PAD + (n + 1) * 512],
                                      start=True, stop=True)
                mm.then_inc(pool_mm, 1)

            pe.wait_ge(v_ready, 6)
            pe.wait_ge(proj_out, PROJ.index((ORDER.index(3), 1)) + 1)
            pe.wait_ge(const_in, 16 * 9)
            for u, tick in enumerate(ticks):
                if u < NU and u % 2 == 0:
                    scores(u)
                    scores(u + 1)
                if u == 1:
                    pe.wait_ge(proj_out, 2 * MT)
                if u == NU + POOL_LAG:
                    pe.wait_ge(bias_done, NU)
                    for i in range(2):
                        for n in range(2):
                            pooled(i, n)
                for kind, s, c in tick:
                    (transposes if kind == "T" else times_values)(s, c)

            def out_proj(n, t):
                g = n * TT + t
                pe.wait_ge(oTlo_done, t + 1)
                pe.wait_ge(pool_out, 4)
                if g >= 4:
                    pe.wait_ge(x1_done, g - 3)
                rows = slice(t * P, (t + 1) * P)
                for k in range(KT):
                    if t == 0:
                        pe.wait_ge(wolo_done[n], k + 1)
                    nc.tensor.matmul(ps[:, g % 4, :], oThi[:, k, rows], wohi[n][:, k, :], start=(k == 0), stop=False)
                    nc.tensor.matmul(ps[:, g % 4, :], oThi[:, k, rows], wolo[n][:, k, :], start=False, stop=False)
                    mm = nc.tensor.matmul(ps[:, g % 4, :], oTlo[:, k, rows], wohi[n][:, k, :], start=False, stop=(k == KT - 1))
                mm.then_inc(out_mm, 1)

            def h2_transposes(t):
                pe.wait_ge(h2_done, t + 1)
                if t >= 1:
                    pe.wait_ge(h2T_done, 2 * t)
                for j in range(2):
                    for c in range(4):
                        k = 4 * j + c
                        mm = nc.tensor.transpose(ps[:, 4 + j, c * P:(c + 1) * P], h2[t % 2][:, k * P:(k + 1) * P], ident[:])
                    mm.then_inc(h2tr_done, 1)

            def logits(t):
                pe.wait_ge(h2T_done, 2 * t + 2)
                if t >= 2:
                    pe.wait_ge(logit_done, t - 1)
                for k in range(KT):
                    mm = nc.tensor.matmul(ps[:, 6 + t % 2, 0:NR], h2T[t % 2][:, k, :], rw[:, k, :],
                                          start=(k == 0), stop=(k == KT - 1))
                mm.then_inc(logit_mm, 1)

            for t in range(TT):
                out_proj(0, t)
            for t in range(TT):
                out_proj(1, t)
                if t >= 2:
                    h2_transposes(t - 2)
                if t >= 3:
                    logits(t - 3)
            h2_transposes(TT - 2)
            logits(TT - 3)
            h2_transposes(TT - 1)
            logits(TT - 2)
            logits(TT - 1)
            pe.wait_ge(rd, RD_COUNTED)
            nc.tensor.matmul(ps[:, 0, 0:TT * N_EXP], ut[:], rt[2][:].rearrange("p t e -> p (t e)"), start=True, stop=False)
            nc.tensor.matmul(ps[:, 0, 0:TT * N_EXP], ones[:], rt[3][:].rearrange("p t e -> p (t e)"), start=False, stop=True)
            nc.tensor.matmul(ps[:, 1, 0:N_EXP], ones[:], rs[:, 20, :], start=True, stop=True).then_inc(rank_mm, 1)

            for c in range(2 * TT):
                pe.wait_ge(one_hots, 2 * c + 2)
                mm = nc.tensor.matmul(ps[0:CAP, 2, 0:LT], row_hot[:, c, :], tile_hot[:, c, :], start=(c == 0), stop=(c == 2 * TT - 1))
            mm.then_inc(list_mm, 1)

            def ex_transposes(e, u, src, first):
                for k in range(KT):
                    mm = nc.tensor.transpose(ps[:, k // 4, (k % 4) * COLS:(k % 4 + 1) * COLS],
                                             src[:, k * P:(k + 1) * P], ident[0:COLS, 0:COLS])
                return mm

            def gate_up(u, bank, xTu):
                for f in range(4):
                    w = (wg if f < 2 else wu)[u]
                    c0 = (f % 2) * P
                    for k in range(KT):
                        mm = nc.tensor.matmul(ps[:, bank, f * COLS:(f + 1) * COLS], w[:, k, c0:c0 + P], xTu[:, k, :],
                                              start=(k == 0), stop=(k == KT - 1))
                return mm

            def down(u, b0, hTu):
                for n in range(2):
                    for j in range(2):
                        mm = nc.tensor.matmul(ps[0:CAP, b0 + n, :], hTu[:, j, 0:CAP], wd[u][:, j, n * 512:(n + 1) * 512],
                                              start=(j == 0), stop=(j == 1))
                return mm

            def down_split(slot, par, e):
                pe.wait_ge(hT_done, e + 1)
                pe.wait_ge(wdlo_done, e + 1)
                b0 = 4 + 2 * par
                for n in range(2):
                    cols = slice(n * 512, (n + 1) * 512)
                    for j in range(2):
                        nc.tensor.matmul(ps[0:CAP, b0 + n, :], hThi_e[par][:, j, :], wdhi[par][:, j, cols], start=(j == 0), stop=False)
                        nc.tensor.matmul(ps[0:CAP, b0 + n, :], hThi_e[par][:, j, :], wdlo[slot][:, j, cols], start=False, stop=False)
                    if n == 0:
                        pe.wait_ge(hTlo_done, e + 1)
                    for j in range(2):
                        mm = nc.tensor.matmul(ps[0:CAP, b0 + n, :], hTlo_e[par][:, j, :], wdhi[par][:, j, cols], start=False, stop=(j == 1))
                return mm

            def expert(it, u):
                first = isinstance(it, int)
                e = it * RING + u
                pe.wait_ge(xg_in[u % 2], 16 * (u // 2 + 1) + it * (16 * RING // 2))
                if not first or u >= 1:
                    pe.wait_ge(xT_done, e)
                ex_transposes(e, u, xg[u % 2], first).then_inc(etr_done, 1)
                if not first or u >= 2:
                    down_of(e - 2, (u - 2) % RING, u % 2, first)
                pe.wait_ge(xT_done, e + 1)
                pe.wait_ge(wgu_in[u], it * 32 + 32)
                if not first or u >= 2:
                    pe.wait_ge(hT_done, e - 1)
                gate_up(u, 2 + u % 2, xT[u % 2]).then_inc(gu_done, 1)

            def down_of(e, slot, par, early):
                if not early:
                    pe.wait_ge(y_a, e - 1)
                    pe.wait_ge(y_v, e - 1)
                down_split(slot, par, e).then_inc(down_done, 1)

            for u in range(RING):
                expert(0, u)
            with pe.Fori(1, N_EXP // RING) as it:
                for u in range(RING):
                    expert(it, u)
            for e in (N_EXP - 2, N_EXP - 1):
                down_of(e, e % RING, e % 2, False)

            n_ovf = pe.value_load(eid[0:1, N_OVF:N_OVF + 1], min_val=0, max_val=N_OVF)
            pe.wait_ge(xT_done, N_EXP)
            pe.wait_ge(hT_done, N_EXP)
            pe.wait_ge(y_a, N_EXP)
            pe.wait_ge(y_v, N_EXP)
            with pe.If(n_ovf > 0):
                with pe.Fori(0, N_OVF) as j:
                    with pe.If(j < n_ovf):
                        pe.wait_ge(v_x, j * 16 + 16)
                        ex_transposes(0, 0, xg[0], False).then_inc(v_tr, 1)
                        pe.wait_ge(v_xT, j + 1)
                        pe.wait_ge(v_w, j * 48 + 48)
                        gate_up(0, 2, xT[0]).then_inc(v_gu, 1)
                        pe.wait_ge(v_hT, j + 1)
                        down(0, 4, hT[0]).then_inc(down_done, 1)

        @block.scalar
        def _(act):
            def square(t):
                act.wait_ge(x_in[t % NX], 16 * (t // NX + 1))
                if t >= NX:
                    act.wait_ge(xtr_done, 2 * (t - NX + 1))
                nc.scalar.activation(xn[t % NX][:], xin[t % NX][:], ACT.Square, scale=D ** -0.5, accum_out=stat[:, 0, t:t + 1]).then_inc(sq_done, 1)

            def high(t):
                for j in range(2):
                    b = 2 * t + j
                    act.wait_ge(xtr_done, b + 1)
                    nc.scalar.copy(hThi[:, 4 * j:4 * j + 4, t * P:(t + 1) * P],
                                   ps[:, b % 4, :].rearrange("p (c q) -> p c q", c=4)).then_inc(hi_done, 1)

            def projected(i, n):
                m, g = ORDER[i], PROJ.index((i, n))
                act.wait_ge(proj_done, g + 1)
                bank = ps[:, 4 + g % 4, :]
                cols = slice(n * 512, (n + 1) * 512)
                if m in V_TILES:
                    v = V_TILES.index(m)
                    if v >= 2:
                        act.wait_ge(vtr_done, 2)
                    nc.scalar.copy(vT[v % 2][:, cols], bank).then_inc(proj_out, 1)
                elif m < 2:
                    nc.scalar.mul(qa[:, m, cols], bank, -(HD ** -0.5)).then_inc(proj_out, 1)
                elif m < 4:
                    nc.scalar.copy(ka[:, m - 2, cols], bank).then_inc(proj_out, 1)
                elif m < 10:
                    nc.scalar.mul(qb[:, m - 6, cols], bank, -(HD ** -0.5)).then_inc(proj_out, 1)
                elif m == 10:
                    for gg in range(2):
                        for side in range(2):
                            a = nc.scalar.copy(kb[side * HD:(side + 1) * HD, gg, cols], bank[gg * HD:(gg + 1) * HD, :])
                    a.then_inc(proj_out, 1)
                else:
                    nc.scalar.copy(cu[:, m - 12, PAD + n * 512:PAD + (n + 1) * 512], bank).then_inc(proj_out, 1)

            def w_high(i):
                act.wait_ge(w_in_s[0], 8 * i + 16)
                if i == 2:
                    act.wait_ge(proj_done, PROJ.index((0, 1)) + 1)
                    act.wait_ge(w_split, 4)
                nc.scalar.copy(whi[0][:], wraw[0][:]).then_inc(w_split, 1)

            for t in range(NX):
                square(t)
            high(0)
            w_high(0)
            for t in range(1, 4):
                high(t)
                square(t + NX - 1)
            square(TT - 1)
            high(4)
            high(5)
            projected(0, 0)
            high(6)
            high(7)
            for i, n in PROJ[1:3]:
                projected(i, n)
            w_high(2)
            for i, n in PROJ[3:]:
                projected(i, n)

            def exponentials(u):
                s = u // 4
                act.wait_ge(bias_done, u + 1)
                buf = pbuf(u)
                if s >= NA_STEPS:
                    buf = pswa[s % 4][:, u % 4, 0:1 + steps[s][4]]
                nc.scalar.activation(buf, buf, ACT.Exp, bias=mneg[:, u:u + 1], scale=-1.0,
                                     accum_out=esum[:, u:u + 1]).then_inc(exp_done, 1)

            def o_evacuate(s):
                kind, i, g, _, _ = steps[s]
                oi = o_steps.index(s)
                act.wait_ge(pv_done, vnum[(s, last_chunk[s])] + 1)
                bank = ps[:, 6 + oi % 2, :]
                if kind == "na":
                    dst, src = oT[:, 0:2, i * P:(i + 1) * P], bank[:, 0:2 * P].rearrange("p (t q) -> p t q", t=2)
                else:
                    dst, src = oT[:, 2:6, i * P:(i + 1) * P], bank.rearrange("p (t q) -> p t q", t=4)
                nc.scalar.copy(dst, src).then_inc(o_out, 1)

            def wo_high(n, k):
                c = n * KT + k
                act.wait_ge(wo_in[wo_buf(c)], 32 * max(c // 4, 1))
                nc.scalar.copy(wohi[n][:, k, :], woraw[wo_buf(c)][:]).then_inc(wohi_done[n], 1)

            def queries_high(b, side):
                rows = slice(side * HD, (side + 1) * HD)
                nc.scalar.copy(qs[b % 2][rows, side::2, :], qb[rows, :, b * P:(b + 1) * P]).then_inc(qhi_done, 1)

            pending = []
            for u, tick in enumerate(ticks):
                if u < NU:
                    exponentials(u)
                g = u - 4 * NA_STEPS - 1
                if g in range(SWA_KV):
                    act.wait_ge(bias_done, 4 * NA_STEPS)
                    act.wait_ge(score_done, 4 * NA_STEPS)
                    nc.scalar.copy(khi[:, g, :], kb[:, g, :]).then_inc(khi_done, 1)
                b, side = split_block(u)
                if b:
                    if b > 2:
                        act.wait_ge(score_done, 4 * NA_STEPS + 8 * (b - 1))
                    queries_high(b, side)
                if u == NU + POOL_LAG:
                    act.wait_ge(const_in, 16 * 9)
                    for i in range(2):
                        for n in range(2):
                            act.wait_ge(pool_mm, 2 * i + n + 1)
                            nc.scalar.mul(oT[:, 6 + i, n * 512:(n + 1) * 512], ps[:, 2 * i + n, :],
                                          pscale[:, i:i + 1]).then_inc(pool_out, 1)
                for s in pending:
                    o_evacuate(s)
                pending = []
                for kind, s, c in tick:
                    if kind == "T" and not by_vector(chunk_no[(s, c)]):
                        evacuate_chunk(act, nc.scalar.copy, pt_a, s, c)
                    if kind == "T" and chunk_no[(s, c)] == len(chunk_no) - 1:
                        act.wait_ge(tr_done, len(chunk_no))
                        wo_high(0, 0)
                        wo_high(0, 1)
                    if kind == "V" and c == last_chunk[s]:
                        pending.append(s)
            for s in pending:
                o_evacuate(s)

            def oT_high(t):
                nc.scalar.copy(oThi[:, :, t * P:(t + 1) * P], oT[:, :, t * P:(t + 1) * P]).then_inc(oThi_done, 1)

            act.wait_ge(pool_out, 4)
            act.wait_ge(o_out, len(o_steps))
            oT_high(0)
            for k in range(2, KT):
                wo_high(0, k)
            for t in range(1, TT):
                oT_high(t)

            def square2(t):
                act.wait_ge(x1_done, TT + t + 1)
                if t >= 2:
                    act.wait_ge(h2tr_done, 2 * (t - 1))
                    act.wait_ge(h2_stored[t % 2], 16 * (t // 2))
                nc.scalar.activation(h2[t % 2][:], x1[:, t, :], ACT.Square, scale=D ** -0.5, accum_out=stat[:, 2, t:t + 1]).then_inc(sq2_done, 1)

            def h2T_copy(t):
                for j in range(2):
                    act.wait_ge(h2tr_done, 2 * t + j + 1)
                    if t >= 2 and j == 0:
                        act.wait_ge(logit_mm, t - 1)
                    nc.scalar.copy(h2T[t % 2][:, 4 * j:4 * j + 4, :],
                                   ps[:, 4 + j, :].rearrange("p (c q) -> p c q", c=4)).then_inc(h2T_done, 1)

            for t in range(TT):
                square2(t)
                if t >= 2:
                    h2T_copy(t - 2)
            h2T_copy(TT - 2)
            h2T_copy(TT - 1)
            act.wait_ge(rd, RD_GROUP)
            nc.scalar.activation(rs[:, 1, :], rs[:, 0, :], ACT.Exp).then_inc(r_exp, 1)
            act.wait_ge(rd, RD_PAIR)
            nc.scalar.activation(rs[:, 9, 0:TT], rs[:, 8, 0:TT], ACT.Exp).then_inc(r_exp, 1)

            def xT_copy(dst):
                return nc.scalar.copy(dst[:].rearrange("p (b c) q -> p b c q", b=2),
                                      ps[:, 0:2, 0:4 * COLS].rearrange("p b (c q) -> p b c q", c=4))

            def silu(dst, bank):
                return nc.scalar.activation(dst[:], ps[:, bank, 0:2 * COLS].rearrange("p (f q) -> p f q", f=2), ACT.Silu)

            def expert(it, u):
                first = isinstance(it, int)
                e = it * RING + u
                act.wait_ge(etr_done, e + 1)
                if not first or u >= 2:
                    act.wait_ge(gu_done, e - 1)
                xT_copy(xT[u % 2]).then_inc(xT_done, 1)
                if not first or u >= 2:
                    y_low(it, u)
                act.wait_ge(wd_in[u], it * 16 + 16)
                if not first or u >= 2:
                    act.wait_ge(down_done, e - 1)
                elif u == 0:
                    act.wait_ge(tok_done, 2)
                nc.scalar.copy(wdhi[u % 2][:], wd[u][:]).then_inc(wdhi_done, 1)
                act.wait_ge(gu_done, e + 1)
                silu(sg[u % 2], 2 + u % 2).then_inc(silu_done, 1)

            def y_low(it, u):
                e = it * RING + u
                par = u % 2
                act.wait_ge(down_done, e - 1)
                if not (isinstance(it, int) and it == 0):
                    act.wait_ge(y_put[par], put_count(it, u - 2))
                nc.scalar.copy(ysb[par][:, 0:512], ps[0:CAP, 4 + 2 * par, :]).then_inc(y_a, 1)

            for u in range(RING):
                expert(0, u)
            with act.Fori(1, N_EXP // RING) as it:
                for u in range(RING):
                    expert(it, u)
            y_low(N_EXP // RING, 0)
            y_low(N_EXP // RING, 1)

            n_ovf = act.value_load(eid[0:1, N_OVF:N_OVF + 1], min_val=0, max_val=N_OVF)
            with act.If(n_ovf > 0):
                with act.Fori(0, N_OVF) as j:
                    with act.If(j < n_ovf):
                        act.wait_ge(v_tr, j + 1)
                        xT_copy(xT[0]).then_inc(v_xT, 1)
                        act.wait_ge(v_gu, j + 1)
                        silu(sg[0], 2).then_inc(v_silu, 1)
                        act.wait_ge(down_done, j + (N_EXP + 1))
                        act.wait_ge(y_put[0], j * 16 + 16 * (N_EXP // 2))
                        nc.scalar.copy(ysb[0][:, 0:512], ps[0:CAP, 4, :]).then_inc(v_ya, 1)

            for t in range(TT):
                act.wait_ge(c_sum, 2 * (t + 1))
                nc.scalar.activation(fo[t][:], x1[:, t, :], ACT.Square, scale=D ** -0.5, accum_out=stat[:, 0, t:t + 1]).then_inc(c_sq_done, 1)

        @block.vector
        def _(dve):
            def normalise(t):
                dve.wait_ge(rstd_a, t + 1)
                dve.wait_ge(x_in[t % NX], 16 * (t // NX + 1))
                nc.vector.scalar_tensor_tensor(out=xn[t % NX][:], in0=xin[t % NX][:], scalar=stat[:, 1, t:t + 1], in1=gbc[:],
                                               op0=ALU.mult, op1=ALU.mult).then_inc(xn_done, 1)

            def low(t):
                for j in range(2):
                    b = 2 * t + j
                    dve.wait_ge(hi_done, b + 1)
                    nc.vector.tensor_tensor(hTlo[:, 4 * j:4 * j + 4, t * P:(t + 1) * P],
                                            ps[:, b % 4, :].rearrange("p (c q) -> p c q", c=4),
                                            hThi[:, 4 * j:4 * j + 4, t * P:(t + 1) * P].bitcast(F32),
                                            ALU.subtract).then_inc(lo_done, 1)

            def values(v):
                for n in range(2):
                    dve.wait_ge(vtr_done, 2 * v + n + 1)
                    nc.vector.tensor_copy(vtok[:, 4 * n:4 * n + 4, v * P:(v + 1) * P],
                                          ps[:, (2 * v + n) % 4, :].rearrange("p (c q) -> p c q", c=4)).then_inc(v_ready, 1)

            def w_low(i):
                dve.wait_ge(w_split, 2 * i + 1)
                nc.vector.tensor_tensor(wlo[0][:], wraw[0][:], whi[0][:].bitcast(F32), ALU.subtract).then_inc(w_split, 1)

            nc.vector.memset(cu[:, :, 0:PAD], 0.0).then_inc(cu_zero, 1)
            nc.vector.memset(cu[:, :, PAD + S:PAD + S + PAD], 0.0).then_inc(cu_zero, 1)
            nc.vector.memset(pwd[:], 0.0).then_inc(cu_zero, 1)
            dve.wait_ge(g_in, 16)
            for t in range(3):
                normalise(t)
            low(0)
            normalise(3)
            low(1)
            w_low(0)
            low(2)
            low(3)
            normalise(4)
            normalise(5)
            for t in range(4, TT):
                low(t)
                if t + 2 < TT:
                    normalise(t + 2)
            w_low(2)
            dve.wait_ge(tab_in, 16 * 3)
            dve.wait_ge(cmask_in, 32)
            dve.wait_ge(cu_zero, 3)
            nc.vector.tensor_tensor(te[:].rearrange("p h r c -> p (h r) c"),
                                    colmask[:].unsqueeze(1).to_broadcast([P, NA_HEADS * NEDGE, GRID_W]),
                                    te[:].rearrange("p h r c -> p (h r) c"), ALU.subtract).then_inc(te_ready, 1)
            dve.wait_ge(te_ready, 1)
            for h in range(NA_HEADS):
                nc.vector.tensor_tensor(ti[:, h], te[:, h, 2:2 + NINNER, :],
                                        rowmask[:].unsqueeze(2).to_broadcast([P, NINNER, GRID_W]), ALU.add).then_inc(ti_ready, 1)
            dve.wait_ge(const_in, 16 * 9)
            nc.vector.tensor_scalar(nsink[:], nsink[:], -1.0, None, ALU.mult).then_inc(sink_set, 1)
            for v in range(3):
                values(v)

            dve.wait_ge(proj_done, 2 * MT)
            dve.wait_ge(ti_ready, NA_HEADS)
            dve.wait_ge(sink_set, 1)

            def bias_and_max(u):
                s, h = u // 4, u % 4
                kind, i, g, k0, nk = steps[s]
                dve.wait_ge(score_done, u + 1)
                if kind == "na":
                    if h == 0 and s >= 3:
                        dve.wait_ge(tr_done, chunk_no[(s - 3, last_chunk[s - 3])] + 1)
                    rows = nk // GRID_W
                    r0 = k0 // GRID_W - 2 * i
                    inner = rows == 9
                    tab = ti[:, h, 0:9, :] if inner else te[:, h, r0 + 6:r0 + 6 + rows, :]
                    nc.vector.tensor_tensor_reduce(
                        out=pbuf(u).rearrange("p (b k) -> p b k", b=2), in0=ps[:, sbank(u):sbank(u) + 2, 0:nk // 2],
                        in1=tab.rearrange("p r c -> p (r c)").rearrange("p (b k) -> p b k", b=2),
                        scale=1.0, scalar=BIG, op0=ALU.add, op1=ALU.min, accum_out=mneg[:, u:u + 1]).then_inc(bias_done, 1)
                else:
                    hh = 4 * g + h
                    if h == 0:
                        before = s - 4 if s >= NA_STEPS + 4 else (5, 5, 6, 7)[s - NA_STEPS]
                        dve.wait_ge(tr_done, chunk_no[(before, last_chunk[before])] + 1)
                        nc.vector.tensor_copy(pswa[s % 4][:, :, 0], nsink[:, 4 * g:4 * g + 4]).then_inc(sink_set, 1)
                        dve.wait_ge(sink_set, 2 + s - NA_STEPS)
                    first = (k0 // P) - (i - 1)
                    nc.vector.tensor_tensor_reduce(
                        out=pbuf(u), in0=ps[:, sbank(u), 0:nk], in1=alibi[:, hh, first * P:first * P + nk],
                        scale=1.0, scalar=nsink[:, hh:hh + 1], op0=ALU.add, op1=ALU.min,
                        accum_out=mneg[:, u:u + 1]).then_inc(bias_done, 1)

            def reciprocal(u):
                dve.wait_ge(exp_done, u + 1)
                nc.vector.reciprocal(esum[:, u:u + 1], esum[:, u:u + 1]).then_inc(recip_done, 1)

            def queries_low(b, side):
                rows, other = slice(side * HD, (side + 1) * HD), slice((1 - side) * HD, (2 - side) * HD)
                dve.wait_ge(qhi_done, 2 * (b - 1) + side + 1)
                nc.vector.tensor_tensor(qs[b % 2][other, side::2, :], qb[rows, :, b * P:(b + 1) * P],
                                        qs[b % 2][rows, side::2, :].bitcast(F32), ALU.subtract).then_inc(qlo_done, 1)

            for u, tick in enumerate(ticks):
                if u < NU:
                    bias_and_max(u)
                b, side = split_block(u - 1)
                if b:
                    queries_low(b, side)
                if 0 <= u - 1 < NU:
                    reciprocal(u - 1)
                    if norm_by_vector(u - 1):
                        dve.wait_ge(recip_done, u)
                        nc.vector.tensor_scalar(pbuf(u - 1), pbuf(u - 1), esum[:, u - 1:u], None, ALU.mult).then_inc(norm_v, 1)
                for kind, s, c in tick:
                    if kind == "T" and by_vector(chunk_no[(s, c)]):
                        evacuate_chunk(dve, nc.vector.tensor_copy, pt_v, s, c)

            def wo_low(n, k):
                c = n * KT + k
                dve.wait_ge(wohi_done[n], k + 1)
                nc.vector.tensor_tensor(wolo[n][:, k, :], woraw[wo_buf(c)][:], wohi[n][:, k, :].bitcast(F32),
                                        ALU.subtract).then_inc(wolo_done[n], 1)

            def oT_low(t):
                dve.wait_ge(oThi_done, t + 1)
                nc.vector.tensor_tensor(oTlo[:, :, t * P:(t + 1) * P], oT[:, :, t * P:(t + 1) * P],
                                        oThi[:, :, t * P:(t + 1) * P].bitcast(F32), ALU.subtract).then_inc(oTlo_done, 1)

            for k in range(KT):
                wo_low(0, k)
                if k == 0:
                    oT_low(0)
            for t in range(1, TT):
                oT_low(t)

            def residual(g):
                n, t = g // TT, g % TT
                dve.wait_ge(out_mm, g + 1)
                dve.wait_ge(xr_in[g % 2], 16 * (g // 2 + 1))
                nc.vector.tensor_tensor(x1[:, t, n * 512:(n + 1) * 512], ps[:, g % 4, :], xres[g % 2][:], ALU.add).then_inc(x1_done, 1)

            def normalise2(t):
                dve.wait_ge(rstd_b, t + 1)
                nc.vector.scalar_tensor_tensor(out=h2[t % 2][:], in0=x1[:, t, :], scalar=stat[:, 3, t:t + 1], in1=gbc[:],
                                               op0=ALU.mult, op1=ALU.mult).then_inc(h2_done, 1)

            def take_logits(t):
                dve.wait_ge(logit_mm, t + 1)
                nc.vector.tensor_tensor(logit[:, t, :], ps[:, 6 + t % 2, 0:NR], rb[:], ALU.add).then_inc(logit_done, 1)

            dve.wait_ge(g_in, 32)
            for g in range(TT):
                residual(g)
            for t in range(TT):
                residual(TT + t)
                normalise2(t)
                if t >= 3:
                    take_logits(t - 3)
            for t in range(TT - 3, TT):
                take_logits(t)

            count = [0]

            def step(ins):
                count[0] += 1
                ins.then_inc(rd, 1)
                dve.wait_ge(rd, count[0])

            def steps_apart(*several):
                for ins in several:
                    count[0] += 1
                    ins.then_inc(rd, 1)
                dve.wait_ge(rd, count[0])

            v = nc.vector
            B8 = lambda a, n: a.unsqueeze(2).to_broadcast([P, TT, n])
            gl, el = logit[:, :, 0:N_GROUPS], logit[:, :, N_GROUPS:NR]
            w4 = misc[:, 0:4].unsqueeze(1).to_broadcast([P, TT, 4])
            w8 = misc[:, 4:12].unsqueeze(1).to_broadcast([P, TT, 8])
            iota_e = misc[:, 12:44].unsqueeze(1).to_broadcast([P, TT, N_EXP])
            iota_j = misc[:, 12:12 + N_OVF].unsqueeze(2).to_broadcast([P, N_OVF, N_EXP])
            s8 = lambda i: rs[:, i, 0:TT]
            s32 = lambda i, n: rs[:, i, 0:TT * n].rearrange("p (t n) -> p t n", t=TT)
            s64 = lambda i: rs[:, i:i + 2, :].rearrange("p a (t n) -> p (a t) n", n=8)
            dve.wait_ge(logit_done, TT)

            def first_of_best(values, best, weights, hot, top, n):
                step(v.tensor_tensor(hot, values, B8(best, n), ALU.is_ge))
                step(v.tensor_tensor(hot, hot, weights, ALU.mult))
                step(v.tensor_reduce(top, hot, AX_X, ALU.max))
                step(v.tensor_tensor(hot, hot, B8(top, n), ALU.is_equal))

            step(v.tensor_reduce(s8(2), gl, AX_X, ALU.max))
            step(v.tensor_tensor(s32(0, 4), gl, B8(s8(2), 4), ALU.subtract))
            assert count[0] == RD_GROUP
            first_of_best(gl, s8(2), w4, s32(3, 4), s8(4), 4)
            hotg = s32(3, 4).unsqueeze(3).to_broadcast([P, TT, 4, 8])
            step(v.tensor_tensor(rt[0][:].rearrange("p t (g e) -> p t g e", g=4),
                                 el.rearrange("p t (g e) -> p t g e", g=4), hotg, ALU.mult))
            step(v.tensor_reduce(s64(5), rt[0][:].rearrange("p t (g e) -> p t e g", g=4), AX_X, ALU.add))
            step(v.tensor_reduce(s8(7), s64(5), AX_X, ALU.max))
            first_of_best(s64(5), s8(7), w8, s64(10), s8(12), 8)
            step(v.scalar_tensor_tensor(out=s64(5), in0=s64(10), scalar=-BIG, in1=s64(5), op0=ALU.mult, op1=ALU.add))
            step(v.tensor_reduce(s8(13), s64(5), AX_X, ALU.max))
            step(v.tensor_tensor(s8(8), s8(13), s8(7), ALU.subtract))
            assert count[0] == RD_PAIR
            first_of_best(s64(5), s8(13), w8, s64(14), s8(12), 8)
            for k, hot in enumerate((s64(10), s64(14))):
                step(v.tensor_tensor(rt[k][:].rearrange("p t (g e) -> p t g e", g=4), hotg,
                                     hot.unsqueeze(2).to_broadcast([P, TT, 4, 8]), ALU.mult))
            step(v.tensor_tensor(rt[2][:], rt[0][:], rt[1][:], ALU.add))
            step(v.memset(rt[3][:, 0, :], 0.0))
            for t in range(1, TT):
                step(v.tensor_tensor(rt[3][:, t, :], rt[3][:, t - 1, :], rt[2][:, t - 1, :], ALU.add))
            step(v.tensor_tensor(rs[:, 20, :], rt[3][:, TT - 1, :], rt[2][:, TT - 1, :], ALU.add))
            assert count[0] == RD_COUNTED
            dve.wait_ge(r_exp, 2)
            step(v.tensor_reduce(s8(2), s32(1, 4), AX_X, ALU.add))
            step(v.reciprocal(s8(2), s8(2)))
            step(v.tensor_scalar(s8(4), s8(9), 1.0, None, ALU.add))
            step(v.reciprocal(s8(4), s8(4)))
            step(v.tensor_tensor(gates[:, 0, :], s8(2), s8(4), ALU.mult))
            step(v.tensor_tensor(gates[:, 1, :], gates[:, 0, :], s8(9), ALU.mult))
            dve.wait_ge(rank_mm, 1)
            rank = ps[:, 0, 0:TT * N_EXP].rearrange("p (t e) -> p t e", t=TT)
            steps_apart(v.tensor_scalar(rs[:, 16, :], ps[:, 1, 0:N_EXP], 1.0 / CAP, (CAP - 0.5) / CAP - 0.5, ALU.mult, ALU.add),
                        v.tensor_scalar(rt[4][:], rank, 1.0 / CAP, 0.5 / CAP - 0.5, ALU.mult, ALU.add))
            steps_apart(v.tensor_scalar(rs[:, 16, :], rs[:, 16, :], MAGIC, None, ALU.add),
                        v.tensor_scalar(rt[4][:], rt[4][:], MAGIC, None, ALU.add))
            steps_apart(v.tensor_scalar(rs[:, 16, :], rs[:, 16, :], MAGIC + 1.0, 0.0, ALU.subtract, ALU.max),
                        v.tensor_scalar(rt[4][:], rt[4][:], MAGIC, None, ALU.subtract))
            a, b = 16, 17
            sh = 1
            while sh < N_EXP:
                steps_apart(v.tensor_copy(rs[:, b, 0:sh], rs[:, a, 0:sh]),
                            v.tensor_tensor(rs[:, b, sh:], rs[:, a, sh:], rs[:, a, 0:N_EXP - sh], ALU.add))
                a, b = b, (18 if b == 17 else 17)
                sh *= 2
            incl = rs[:, a, :]
            step(v.tensor_tensor(rs[:, 19, :], incl, rs[:, 16, :], ALU.subtract))
            step(v.tensor_scalar(rs[:, 19, :], rs[:, 19, :], N_EXP - 1.0, None, ALU.add))
            steps_apart(v.scalar_tensor_tensor(out=rt[5][:], in0=rt[4][:], scalar=-float(CAP), in1=rank, op0=ALU.mult, op1=ALU.add),
                        v.tensor_tensor(rt[6][:], rt[4][:], rs[:, 19, :].unsqueeze(1).to_broadcast([P, TT, N_EXP]), ALU.add))
            steps_apart(v.tensor_tensor(rt[6][:], rt[6][:], iota_e, ALU.subtract),
                        v.tensor_scalar(rt[4][:], rt[4][:], 1.0, None, ALU.min))
            step(v.tensor_tensor(rt[6][:], rt[6][:], rt[4][:], ALU.mult))
            step(v.tensor_tensor(rt[6][:], rt[6][:], iota_e, ALU.add))
            step(v.scalar_tensor_tensor(out=rt[5][:], in0=rt[5][:], scalar=float(PITCH), in1=rt[6][:], op0=ALU.mult, op1=ALU.add))
            pos, row, tile = place[:, 0, :], place[:, 1, :], place[:, 2, :]
            steps_apart(*[v.tensor_tensor(rt[6 + k][:], rt[k][:], rt[5][:], ALU.mult) for k in range(2)])
            steps_apart(*[v.tensor_reduce(pos[:, k * TT:(k + 1) * TT], rt[6 + k][:], AX_X, ALU.add) for k in range(2)])
            step(v.tensor_scalar(row, pos, 1.0 / PITCH, 0.5 / PITCH - 0.5, ALU.mult, ALU.add))
            step(v.tensor_scalar(row, row, MAGIC, None, ALU.add))
            step(v.tensor_scalar(row, row, MAGIC, None, ALU.subtract))
            step(v.scalar_tensor_tensor(out=tile, in0=row, scalar=-float(PITCH), in1=pos, op0=ALU.mult, op1=ALU.add))
            dve.wait_ge(h2T_done, 2 * TT)
            dve.wait_ge(logit_mm, TT)
            dve.wait_ge(out_mm, 2 * TT)
            dve.wait_ge(pc_in, 16 * 6)
            for c in range(2 * TT):
                v.tensor_scalar(row_hot[:, c, :], misc[:, 12:12 + CAP], row[:, c:c + 1], None, ALU.is_equal).then_inc(one_hots, 1)
                v.tensor_scalar(tile_hot[:, c, :], misc[:, 12:12 + LT], tile[:, c:c + 1], dvals[:, c:c + 1],
                                ALU.is_equal, ALU.mult).then_inc(one_hots, 1)
            step(v.tensor_tensor(ovf_cmp[:], iota_j, incl.unsqueeze(1).to_broadcast([P, N_OVF, N_EXP]), ALU.is_ge))
            step(v.tensor_reduce(rs[:, 21, 0:N_OVF], ovf_cmp[:], AX_X, ALU.add))
            step(v.tensor_scalar(eid[:, 0:N_OVF], rs[:, 21, 0:N_OVF], N_EXP - 1.0, None, ALU.min))
            step(v.tensor_copy(eid[:, N_OVF:N_OVF + 1], incl[:, N_EXP - 1:N_EXP]))
            dve.wait_ge(list_mm, 1)
            entry = ps[0:CAP, 2, 0:LT]
            step(v.tensor_scalar(pad[:], entry, 0.0, NOWHERE - 1.0, ALU.is_equal, ALU.mult))
            step(v.scalar_tensor_tensor(out=dest[:], in0=pad[:], scalar=-1.0, in1=entry, op0=ALU.add, op1=ALU.add))
            nc.vector.tensor_scalar(tok[:], dest[:], float(S), -float(S), ALU.is_ge, ALU.mult).then_inc(tok_done, 1)
            dve.wait_ge(tok_done, 1)
            nc.vector.tensor_tensor(tok[:], tok[:], dest[:], ALU.add).then_inc(tok_done, 1)

            def gated(sgu, dst, bank):
                return nc.vector.tensor_tensor(dst[:], sgu[:], ps[:, bank, 2 * COLS:4 * COLS].rearrange("p (f q) -> p f q", f=2), ALU.mult)

            def y_high(it, u):
                e = it * RING + u
                par = u % 2
                dve.wait_ge(down_done, e - 1)
                if not (isinstance(it, int) and it == 0):
                    dve.wait_ge(y_put[par], put_count(it, u - 2))
                nc.vector.tensor_copy(ysb[par][:, 512:1024], ps[0:CAP, 5 + 2 * par, :]).then_inc(y_v, 1)

            def expert(it, u):
                first = isinstance(it, int)
                e = it * RING + u
                if not first or u >= 2:
                    y_high(it, u)
                dve.wait_ge(wdhi_done, e + 1)
                nc.vector.tensor_tensor(wdlo[u][:], wd[u][:], wdhi[u % 2][:].bitcast(F32), ALU.subtract).then_inc(wdlo_done, 1)
                dve.wait_ge(silu_done, e + 1)
                if not first or u >= 2:
                    dve.wait_ge(down_done, e - 1)
                gated(sg[u % 2], hT[u % 2], 2 + u % 2).then_inc(h_made, 1)
                dve.wait_ge(h_made, e + 1)
                nc.vector.tensor_copy(hThi_e[u % 2][:], hT[u % 2][:, :, 0:CAP]).then_inc(hT_done, 1)
                dve.wait_ge(hT_done, e + 1)
                nc.vector.tensor_tensor(hTlo_e[u % 2][:], hT[u % 2][:, :, 0:CAP], hThi_e[u % 2][:].bitcast(F32),
                                        ALU.subtract).then_inc(hTlo_done, 1)

            for u in range(RING):
                expert(0, u)
            with dve.Fori(1, N_EXP // RING) as it:
                for u in range(RING):
                    expert(it, u)
            y_high(N_EXP // RING, 0)
            y_high(N_EXP // RING, 1)

            n_ovf = dve.value_load(eid[0:1, N_OVF:N_OVF + 1], min_val=0, max_val=N_OVF)
            with dve.If(n_ovf > 0):
                with dve.Fori(0, N_OVF) as j:
                    with dve.If(j < n_ovf):
                        dve.wait_ge(v_silu, j + 1)
                        gated(sg[0], hT[0], 2).then_inc(v_hT, 1)
                        dve.wait_ge(down_done, j + (N_EXP + 1))
                        dve.wait_ge(y_put[0], j * 16 + 16 * (N_EXP // 2))
                        nc.vector.tensor_copy(ysb[0][:, 512:1024], ps[0:CAP, 5, :]).then_inc(v_yv, 1)

            def add_rows(t):
                dve.wait_ge(yc_in[t], 32)
                for k, y in enumerate((y0[t], y1[t])):
                    nc.vector.scalar_tensor_tensor(out=x1[:, t, :], in0=y[:], scalar=gates[:, k, t:t + 1], in1=x1[:, t, :],
                                                   op0=ALU.mult, op1=ALU.add).then_inc(c_sum, 1)
                    dve.wait_ge(c_sum, 2 * t + k + 1)

            def finish(t):
                dve.wait_ge(rstd_a, TT + t + 1)
                nc.vector.scalar_tensor_tensor(out=fo[t][:], in0=x1[:, t, :], scalar=stat[:, 1, t:t + 1], in1=gbc[:],
                                               op0=ALU.mult, op1=ALU.mult).then_inc(c_out, 1)

            dve.wait_ge(g_in, 48)
            add_rows(0)
            for t in range(TT):
                if t + 1 < TT:
                    add_rows(t + 1)
                finish(t)

        @block.gpsimd
        def _(pool):
            gp = nc.gpsimd

            def split(i):
                split_high(i)
                split_low(i)

            def split_high(i):
                pool.wait_ge(w_in_s[i % 2], 16 * (i // 2 + 1))
                if i >= 2:
                    pool.wait_ge(proj_done, PROJ.index((i - 2, 1)) + 1)
                pool.wait_ge(w_split, 2 * i)
                gp.tensor_copy(whi[i % 2][:], wraw[i % 2][:]).then_inc(w_split, 1)

            def split_low(i):
                pool.wait_ge(w_split, 2 * i + 1)
                gp.tensor_tensor(wlo[i % 2][:], wraw[i % 2][:], whi[i % 2][:].bitcast(F32), ALU.subtract).then_inc(w_split, 1)

            gp.memset(neg_half[:], -0.5).then_inc(pad_set, 1)
            pool.wait_ge(pad_set, 1)
            count = [0]

            def inverse_root(src, ready, n, done, t):
                pool.wait_ge(ready, n)
                gp.tensor_scalar(stat[:, src + 1, t:t + 1], stat[:, src, t:t + 1], EPS, None, ALU.add).then_inc(eps_added, 1)
                count[0] += 1
                pool.wait_ge(eps_added, count[0])
                gp.tensor_tensor(stat[:, src + 1, t:t + 1], stat[:, src + 1, t:t + 1], neg_half[:], ALU.pow).then_inc(done, 1)

            for t in range(TT):
                if t == 4:
                    split_high(1)
                inverse_root(0, sq_done, t + 1, rstd_a, t)
                if t == 5:
                    split_low(1)
            pool.dma_start(colmask[:], c_colmask).then_inc(cmask_in, 16)
            pool.dma_start(rowmask[:], c_rowmask).then_inc(cmask_in, 16)
            pool.dma_start(iedge[:], c_iedge).then_inc(pc_in, 16)
            pool.dma_start(dvals[:], c_dest).then_inc(pc_in, 16)
            pool.wait_ge(cu_zero, 3)
            for g in range(4):
                half = slice((g % 2) * HD, (g % 2 + 1) * HD)
                pool.dma_start(pwd[half, g // 2, (g % 2) * HD:(g % 2 + 1) * HD], pool_w[0, g]).then_inc(pc_in, 16)
            for i in range(3, MIX_FROM):
                split(i)

            low, high, full, seq = slice(0, HD), slice(HD, P), slice(0, P), slice(PAD, PAD + S)

            def pair_sum(dst, src, rows, a, b, lo, hi):
                return lambda: gp.tensor_tensor(dst[rows, PAD + lo:PAD + hi], src[rows, PAD + lo + a:PAD + hi + a],
                                                src[rows, PAD + lo + b:PAD + hi + b], ALU.add)

            def means(i):
                c = cu[:, i, :]
                ops = [pair_sum(pa, c, full, -1, 0, -7, S + 8), pair_sum(pb, pa, full, -1, 1, -6, S + 7)]
                if i == 1:
                    ops.append(pair_sum(pa, pb, full, -2, 2, -4, S + 4))
                ops.append(lambda: gp.tensor_copy(pb[low, seq], pa[low, seq]))
                if i == 1:
                    ops.append(pair_sum(pb, pa, high, -4, 4, 0, S))
                ops.append(lambda: gp.tensor_tensor(pb[:, PAD:2 * PAD], pb[:, PAD:2 * PAD], iedge[:, i, 0:PAD], ALU.mult))
                ops.append(lambda: gp.tensor_tensor(pb[:, S:S + PAD], pb[:, S:S + PAD], iedge[:, i, PAD:2 * PAD], ALU.mult))
                ops.append(lambda: gp.tensor_scalar(pb[:, seq], pb[:, seq], iedge[:, i, 2 * PAD:2 * PAD + 1], None, ALU.mult))
                ops.append(lambda: gp.tensor_tensor(c[:, seq], pb[:, seq], c[:, seq], ALU.subtract))
                return ops

            pooling = means(0) + means(1)
            assert len(pooling) == POOL_OPS
            done = 0

            def mix(n):
                nonlocal done
                for _ in range(n):
                    if done < POOL_OPS:
                        pooling[done]().then_inc(pool_step, 1)
                        done += 1
                        pool.wait_ge(pool_step, done)

            for i in range(MIX_FROM, MT):
                split(i)
                if i == MIX_FROM:
                    pool.wait_ge(pc_in, 16 * 6)
                    pool.wait_ge(proj_out, PROJ.index((ORDER.index(13), 1)) + 1)
                    pool.wait_ge(v_ready, 6)
                pool.wait_ge(w_split, 2 * i + 2)
                mix(2)

            pool.wait_ge(proj_out, 2 * MT)
            for u in range(NU):
                if not norm_by_vector(u):
                    pool.wait_ge(recip_done, u + 1)
                    gp.tensor_scalar(pbuf(u), pbuf(u), esum[:, u:u + 1], None, ALU.mult).then_inc(norm_p, 1)
                if u % 5 == 4 and done < POOL_OPS:
                    pool.wait_ge(norm_p, sum(not norm_by_vector(x) for x in range(u + 1)))
                    mix(1)
                if u == KLO_AT:
                    pool.wait_ge(score_done, 4 * NA_STEPS)
                    for g in range(SWA_KV):
                        pool.wait_ge(khi_done, g + 1)
                        gp.tensor_tensor(klo[:, g, :], kb[:, g, :], khi[:, g, :].bitcast(F32), ALU.subtract).then_inc(klo_done, 1)

            pool.wait_ge(oTlo_done, TT)
            for k in range(KT):
                c = KT + k
                pool.wait_ge(wo_in[wo_buf(c)], 32 * max(c // 4, 1))
                gp.tensor_copy(wohi[1][:, k, :], woraw[wo_buf(c)][:]).then_inc(wohi_done[1], 1)
                pool.wait_ge(wohi_done[1], k + 1)
                gp.tensor_tensor(wolo[1][:, k, :], woraw[wo_buf(c)][:], wohi[1][:, k, :].bitcast(F32),
                                 ALU.subtract).then_inc(wolo_done[1], 1)

            for t in range(TT):
                inverse_root(2, sq2_done, t + 1, rstd_b, t)

            for i in range(2):
                pool.wait_ge(h2_stored[i], 16 * (TT // 2))
            pool.wait_ge(h2tr_done, 2 * TT)
            for i in range(2):
                gp.memset(xg[i][:], 0.0).then_inc(xg_zero, 1)

            pool.wait_ge(tok_done, 2)
            pool.wait_ge(xg_zero, 2)

            origin, bound_x, bound_y = (pool.alloc_register(n) for n in ("origin", "bound_x", "bound_y"))
            pool.reg_mov(origin, 0)

            def bound(reg, value):
                pool.reg_add(reg, origin, value)
                return reg

            def gather(it, u):
                first = isinstance(it, int)
                e = it * RING + u
                if not first or u >= 2:
                    pool.wait_ge(etr_done, e - 1)
                    pool.wait_ge(xg_in[u % 2], it * 32 + 16 * (u // 2))
                col = tok[:, u:u + 1] if first else tok[:, bass.ds(e, 1)]
                gp.tensor_copy(tokc[u % 2][:], col).then_inc(idx_t, 1)
                pool.wait_ge(idx_t, e + 1)
                gp.indirect_dma_start(xg[u % 2][0:CAP, :], None, h2_d, bass.IndirectOffsetOnAxis(ap=tokc[u % 2][:].bitcast(U32), axis=0),
                                      bounds_check=bound(bound_x, S - 1), oob_is_err=False).then_inc(xg_in[u % 2], 16)

            def scatter(it, u):
                f = it * RING + u - 3
                par = (u - 3) % 2
                pool.wait_ge(y_a, f + 1)
                pool.wait_ge(y_v, f + 1)
                col = dest[:, f:f + 1] if isinstance(it, int) else dest[:, bass.ds(f, 1)]
                gp.tensor_copy(destc[par][:], col).then_inc(idx_d, 1)
                pool.wait_ge(idx_d, f + 1)
                gp.indirect_dma_start(y_d, bass.IndirectOffsetOnAxis(ap=destc[par][:].bitcast(U32), axis=0), ysb[par][:], None,
                                      bounds_check=bound(bound_y, 2 * S - 1), oob_is_err=False).then_inc(y_put[par], 16)

            for u in range(RING):
                gather(0, u)
            scatter(0, RING - 1)
            with pool.Fori(1, N_EXP // RING) as it:
                for u in range(RING):
                    gather(it, u)
                    scatter(it, u)
            for u in range(3):
                scatter(N_EXP // RING, u)

            n_ovf = pool.value_load(eid[0:1, N_OVF:N_OVF + 1], min_val=0, max_val=N_OVF)
            pool.wait_ge(y_put[0], 16 * (N_EXP // 2))
            pool.wait_ge(etr_done, N_EXP)
            with pool.If(n_ovf > 0):
                with pool.Fori(0, N_OVF) as j:
                    with pool.If(j < n_ovf):
                        pool.wait_ge(y_put[0], j * 16 + 16 * (N_EXP // 2))
                        gp.tensor_copy(tokc[0][:], tok[:, bass.ds(j + N_EXP, 1)]).then_inc(v_idx, 1)
                        gp.tensor_copy(destc[0][:], dest[:, bass.ds(j + N_EXP, 1)]).then_inc(v_idx, 1)
                        pool.wait_ge(v_idx, 2 * j + 2)
                        gp.indirect_dma_start(xg[0][0:CAP, :], None, h2_d, bass.IndirectOffsetOnAxis(ap=tokc[0][:].bitcast(U32), axis=0),
                                              bounds_check=bound(bound_x, S - 1), oob_is_err=False).then_inc(v_x, 16)
                        pool.wait_ge(v_ya, j + 1)
                        pool.wait_ge(v_yv, j + 1)
                        gp.indirect_dma_start(y_d, bass.IndirectOffsetOnAxis(ap=destc[0][:].bitcast(U32), axis=0), ysb[0][:], None,
                                              bounds_check=bound(bound_y, 2 * S - 1), oob_is_err=False).then_inc(y_put[0], 16)
            for t in range(TT):
                inverse_root(0, c_sq_done, t + 1, rstd_a, t)


def constants():
    f = np.float32
    sq = np.stack([np.eye(P), np.ones((P, P)), np.triu(np.ones((P, P)), 1)]).astype(f)
    qc = np.arange(P) % GRID_W
    start = np.clip(qc - NA_COLS // 2, 0, GRID_W - NA_COLS)[:, None]
    kc = np.arange(GRID_W)[None]
    colmask = np.where((kc >= start) & (kc < start + NA_COLS), 0.0, BIG).astype(f)
    rowmask = np.zeros((P, 9), f)
    rowmask[GRID_W:, 0] = BIG
    rowmask[:GRID_W, 8] = BIG
    slopes = (2.0 ** (-8.0 * np.arange(1, SWA_HEADS + 1) / SWA_HEADS)).astype(f)
    diff = np.abs(np.arange(3 * P)[None] - np.arange(P)[:, None] - P).astype(f)
    alibi = np.where(diff[:, None] <= WINDOW, slopes[None, :, None] * diff[:, None], f(BIG)).astype(f)
    iedge = np.zeros((P, 2, 2 * PAD + 2), f)
    t = np.arange(S)
    for g, w in enumerate(POOL_WINDOWS):
        cnt = np.clip(t + w // 2, 0, S) - np.clip(t - w // 2, 0, S)
        rows = slice((g % 2) * HD, (g % 2 + 1) * HD)
        iedge[rows, g // 2, 0:PAD] = w / cnt[:PAD]
        iedge[rows, g // 2, PAD:2 * PAD] = w / cnt[-PAD:]
        iedge[rows, g // 2, 2 * PAD] = 1.0 / w
    misc = np.zeros((1, 12 + NI), f)
    misc[0, 0:4] = np.arange(4, 0, -1)
    misc[0, 4:12] = np.arange(8, 0, -1)
    misc[0, 12:] = np.arange(NI)
    k, tt = np.meshgrid(np.arange(2), np.arange(TT), indexing="ij")
    dvals = (k * S + tt * P).reshape(1, -1) + np.arange(P)[:, None] + 1
    return {"c_sq": sq, "c_colmask": colmask, "c_rowmask": rowmask, "c_alibi": alibi, "c_iedge": iedge,
            "c_misc": misc, "c_dest": dvals.astype(f)}


_INS = ["x", "norm1_g", "w_in", "nat_win", "swa_sink", "pool_w", "pool_scale", "w_out", "norm2_g",
        "router_g_w", "router_g_b", "router_e_w", "router_e_b", "expert_w_gate", "expert_w_up",
        "expert_w_down", "final_g", "c_sq", "c_colmask", "c_rowmask", "c_alibi", "c_iedge", "c_misc", "c_dest"]


def layout(inputs):
    arrays = {k: np.ascontiguousarray(v) for k, v in inputs.items()}
    edge = GRID_W - NA_COLS
    padded = np.pad(arrays.pop("nat_bias")[0], ((0, 0), (0, 0), (edge, edge)))
    arrays["nat_win"] = np.stack([padded[:, :, GRID_W - 1 - q:2 * GRID_W - 1 - q] for q in range(GRID_W)])
    arrays.update(constants())
    return arrays


def kernel(**inputs):
    import concourse.bacc as bacc
    from concourse.bass_utils import run_bass_kernel_spmd

    nc = bacc.Bacc("TRN2", target_bir_lowering=False, num_devices=1)
    arrays = layout(inputs)
    args = [nc.dram_tensor(f"in_{n}", arrays[n].shape, mybir.dt.from_np(arrays[n].dtype), kind="ExternalInput").ap()
            for n in _INS]
    args.append(nc.dram_tensor("out_0", (1, S, D), F32, kind="ExternalOutput").ap())
    encoder(nc, *args)
    r = run_bass_kernel_spmd(nc, [{f"in_{n}": arrays[n] for n in _INS}], core_ids=[0])
    return r.results[0]["out_0"]
```
